# Optimizing a Trainium2 kernel written in Bass

```python
import math
import jax, jax.numpy as jnp
from jax import lax
import numpy as np

D_MODEL = 1024
BATCH = 1
SEQ = 512
DEPTH = 2
DEC_BATCH = 8
DEC_SEQ = 1
PAST_LEN = 256
PAGE_SIZE = 128

N_MIXERS = 2
N_ATT_LAYERS = (DEPTH + N_MIXERS - 1) // N_MIXERS
N_MLSTM_LAYERS = DEPTH // N_MIXERS
EPS = 1e-6

A_HEADS = 8
A_HEAD_DIM = D_MODEL // A_HEADS
A_WIDTH = A_HEADS * A_HEAD_DIM
MOBA_BLOCK = 256
MOBA_TOPK = 3
Q_CHUNK = 32
ROPE_THETA = 10000.0

M_PROJ_FACTOR = 2
M_WIDTH = M_PROJ_FACTOR * D_MODEL
M_HEADS = 4
M_HEAD_DIM = M_WIDTH // M_HEADS
QKV_BLOCK = 4
N_QKV_BLOCKS = M_WIDTH // QKV_BLOCK
CONV_WIDTH = 4
M_CHUNK = 64

kernel_name = "moba_mlstm_hybrid_step"

def rmsnorm(x, g):
    x32 = x.astype(jnp.float32)
    y = x32 * lax.rsqrt(jnp.mean(x32 * x32, axis=-1, keepdims=True) + EPS)
    return (y * g.astype(jnp.float32)).astype(x.dtype)

def rope(x, pos):
    half = x.shape[-1] // 2
    inv = ROPE_THETA ** (-jnp.arange(half, dtype=jnp.float32) / half)
    ang = pos.astype(jnp.float32)[:, None] * inv[None, :]
    cos = jnp.cos(ang)[None, :, None, :]
    sin = jnp.sin(ang)[None, :, None, :]
    x32 = x.astype(jnp.float32)
    x1, x2 = x32[..., :half], x32[..., half:]
    return jnp.concatenate([x1 * cos - x2 * sin, x2 * cos + x1 * sin], axis=-1).astype(x.dtype)

def moba_attention(q, k_all, v_all, q_pos0):
    B, Tq, H, Dh = q.shape
    L = k_all.shape[1]
    scale = Dh ** -0.5
    n_past_blocks = (L - 1) // MOBA_BLOCK
    k_sel = min(MOBA_TOPK, n_past_blocks)
    qc = min(Q_CHUNK, Tq)
    n_chunks = -(-Tq // qc)
    pad_r = n_chunks * qc - Tq
    qp = jnp.pad(q, ((0, 0), (0, pad_r), (0, 0), (0, 0)))
    kp = jnp.pad(k_all, ((0, 0), (MOBA_BLOCK, pad_r), (0, 0), (0, 0)))
    vp = jnp.pad(v_all, ((0, 0), (MOBA_BLOCK, pad_r), (0, 0), (0, 0)))
    q_blk = (q_pos0 + jnp.arange(n_chunks * qc)) // MOBA_BLOCK
    win = MOBA_BLOCK + qc
    if k_sel > 0:
        kb = k_all[:, :n_past_blocks * MOBA_BLOCK].reshape(B, n_past_blocks, MOBA_BLOCK, H, Dh)
        vb = v_all[:, :n_past_blocks * MOBA_BLOCK].reshape(B, n_past_blocks, MOBA_BLOCK, H, Dh)
        k_mean = jnp.mean(kb.astype(jnp.float32), axis=2)
        gate = jnp.einsum('bthd,bjhd->bhtj', qp.astype(jnp.float32), k_mean)
        past_ok = jnp.arange(n_past_blocks)[None, :] < q_blk[:, None]
        gate = jnp.where(past_ok, gate, -jnp.inf)
        _, sel_idx = lax.top_k(gate, k_sel)
        sel_ok = jnp.arange(k_sel)[None, :] < q_blk[:, None]
        kb = kb.transpose(0, 3, 1, 2, 4)
        vb = vb.transpose(0, 3, 1, 2, 4)
    gather_blocks = jax.vmap(jax.vmap(lambda blocks, idx: blocks[idx]))

    def chunk(c):
        q0 = c * qc
        qc_ = lax.dynamic_slice_in_dim(qp, q0, qc, axis=1)
        pos = q_pos0 + q0 + jnp.arange(qc)
        kw = lax.dynamic_slice_in_dim(kp, q_pos0 + q0, win, axis=1)
        vw = lax.dynamic_slice_in_dim(vp, q_pos0 + q0, win, axis=1)
        kpos = q_pos0 + q0 - MOBA_BLOCK + jnp.arange(win)
        own_ok = (kpos[None, :] <= pos[:, None]) & (kpos[None, :] >= (pos[:, None] // MOBA_BLOCK) * MOBA_BLOCK)
        s_own = jnp.einsum('bqhd,bkhd->bhqk', qc_, kw, preferred_element_type=jnp.float32) * scale
        s_own = jnp.where(own_ok, s_own, -jnp.inf)
        if k_sel == 0:
            p = jax.nn.softmax(s_own, axis=-1).astype(vw.dtype)
            return jnp.einsum('bhqk,bkhd->bqhd', p, vw)
        idx = lax.dynamic_slice_in_dim(sel_idx, q0, qc, axis=2)
        ok = lax.dynamic_slice_in_dim(sel_ok, q0, qc, axis=0)
        ks = gather_blocks(kb, idx)
        vs = gather_blocks(vb, idx)
        s_sel = jnp.einsum('bqhd,bhqnkd->bhqnk', qc_, ks, preferred_element_type=jnp.float32) * scale
        s_sel = jnp.where(ok[None, None, :, :, None], s_sel, -jnp.inf)
        n_sel = k_sel * MOBA_BLOCK
        s = jnp.concatenate([s_sel.reshape(B, H, qc, n_sel), s_own], axis=-1)
        p = jax.nn.softmax(s, axis=-1).astype(vw.dtype)
        p_sel = p[..., :n_sel].reshape(B, H, qc, k_sel, MOBA_BLOCK)
        return (jnp.einsum('bhqnk,bhqnkd->bqhd', p_sel, vs)
                + jnp.einsum('bhqk,bkhd->bqhd', p[..., n_sel:], vw))

    out = lax.map(chunk, jnp.arange(n_chunks))
    return jnp.moveaxis(out, 0, 1).reshape(B, n_chunks * qc, H, Dh)[:, :Tq]

def attention_layer(x, q_pos0, k_past, v_past, norm_g, w_in, q_g, k_g, w_out):
    B, T, _ = x.shape
    h = rmsnorm(x, norm_g)
    q, k, v, g = jnp.split(h @ w_in, 4, axis=-1)
    pos = q_pos0 + jnp.arange(T)
    q = rope(rmsnorm(q.reshape(B, T, A_HEADS, A_HEAD_DIM), q_g), pos)
    k = rope(rmsnorm(k.reshape(B, T, A_HEADS, A_HEAD_DIM), k_g), pos)
    v = v.reshape(B, T, A_HEADS, A_HEAD_DIM)
    k_all = k if k_past is None else jnp.concatenate([k_past.astype(k.dtype), k], axis=1)
    v_all = v if v_past is None else jnp.concatenate([v_past.astype(v.dtype), v], axis=1)
    o = moba_attention(q, k_all, v_all, q_pos0).reshape(B, T, A_WIDTH)
    return x + (o * jax.nn.silu(g)) @ w_out, k, v

def mlstm_chunkwise(q, k, v, i_pre, f_pre, C0, n0, m0):
    B, T, _ = q.shape
    L = min(M_CHUNK, T)
    nc = -(-T // L)
    pad = nc * L - T
    f32 = jnp.float32

    def heads(u):
        u = u.astype(f32).reshape(B, T, M_HEADS, M_HEAD_DIM).transpose(0, 2, 1, 3)
        u = jnp.pad(u, ((0, 0), (0, 0), (0, pad), (0, 0)))
        return jnp.moveaxis(u.reshape(B, M_HEADS, nc, L, M_HEAD_DIM), 2, 0)

    def gates(u, fill):
        u = jnp.pad(u.transpose(0, 2, 1), ((0, 0), (0, 0), (0, pad)), constant_values=fill)
        return jnp.moveaxis(u.reshape(B, M_HEADS, nc, L), 2, 0)

    logf = gates(jax.nn.log_sigmoid(f_pre.astype(f32)), 0.0)
    ig = gates(i_pre.astype(f32), -jnp.inf)
    causal = jnp.tril(jnp.ones((L, L), dtype=bool))

    def step(carry, inp):
        C, n, m = carry
        qc, kc, vc, lf, ic = inp
        b = jnp.cumsum(lf, axis=-1)
        Dm = jnp.where(causal, b[..., :, None] - b[..., None, :] + ic[..., None, :], -jnp.inf)
        inter = b + m[..., None]
        m_t = jnp.maximum(inter, jnp.max(Dm, axis=-1))
        S = jnp.einsum('bhtd,bhsd->bhts', qc, kc) * jnp.exp(Dm - m_t[..., None])
        a = jnp.exp(inter - m_t)
        num = jnp.einsum('bhts,bhse->bhte', S, vc) + a[..., None] * jnp.einsum('bhtd,bhde->bhte', qc, C)
        qn = jnp.sum(S, axis=-1) + a * jnp.einsum('bhtd,bhd->bht', qc, n)
        h = num / jnp.maximum(jnp.abs(qn), jnp.exp(-m_t))[..., None]
        m_new = m_t[..., -1]
        decay = jnp.exp(b[..., -1:] - b + ic - m_new[..., None])
        a_end = jnp.exp(b[..., -1] + m - m_new)
        C_new = a_end[..., None, None] * C + jnp.einsum('bhsd,bhse->bhde', kc * decay[..., None], vc)
        n_new = a_end[..., None] * n + jnp.einsum('bhs,bhsd->bhd', decay, kc)
        return (C_new, n_new, m_new), h

    carry0 = (C0.astype(f32), n0.astype(f32), m0.astype(f32))
    (C, n, m), hs = lax.scan(step, carry0, (heads(q), heads(k), heads(v), logf, ig))
    hs = jnp.moveaxis(hs, 0, 2).reshape(B, M_HEADS, nc * L, M_HEAD_DIM)[:, :, :T]
    return hs.transpose(0, 2, 1, 3), C, n, m

def mlstm_layer(x, conv_buf, C0, n0, m0, norm_g, w_in, conv_w, conv_b, w_q, w_k, w_v, w_if, b_if,
                out_g, skip, w_out):
    B, T, _ = x.shape
    h = rmsnorm(x, norm_g)
    xm, og, z = jnp.split(h @ w_in, 3, axis=-1)
    xpad = jnp.concatenate([conv_buf.astype(xm.dtype), xm], axis=1)
    xc = conv_b + sum(xpad[:, j:j + T] * conv_w[j] for j in range(CONV_WIDTH))
    xc = jax.nn.silu(xc)
    new_buf = xpad[:, T:]

    def headwise(u, w):
        u = u.reshape(B, T, N_QKV_BLOCKS, QKV_BLOCK)
        return jnp.einsum('btgi,gio->btgo', u, w).reshape(B, T, M_WIDTH)

    q = headwise(xc, w_q)
    k = headwise(xc, w_k)
    v = headwise(xm, w_v)
    g = jnp.concatenate([q, k, v], axis=-1) @ w_if + b_if
    i_pre, f_pre = g[..., :M_HEADS], g[..., M_HEADS:]
    hc, C, n, m = mlstm_chunkwise(q, k * (M_HEAD_DIM ** -0.5), v, i_pre, f_pre, C0, n0, m0)
    hc = hc * jax.nn.sigmoid(og.astype(jnp.float32)).reshape(B, T, M_HEADS, M_HEAD_DIM)
    mu = jnp.mean(hc, axis=-1, keepdims=True)
    var = jnp.mean(jnp.square(hc - mu), axis=-1, keepdims=True)
    hn = ((hc - mu) * lax.rsqrt(var + EPS)).reshape(B, T, M_WIDTH) * out_g.astype(jnp.float32)
    out = ((hn + skip * xc) * jax.nn.silu(z)).astype(x.dtype)
    return x + out @ w_out, C, n, m, new_buf

def setup_inputs(seed: int = 0) -> dict:
    key = jax.random.key(seed)
    ks = jax.random.split(key, 32)
    f32 = jnp.float32
    n_pages = PAST_LEN // PAGE_SIZE
    n_pool = (DEC_BATCH * n_pages * 5 + 3) // 4

    def nrm(k, shape, s):
        return jax.random.normal(k, shape, f32) * s

    page_table = jax.random.permutation(ks[4], n_pool)[:DEC_BATCH * n_pages]
    page_table = page_table.reshape(DEC_BATCH, n_pages).astype(jnp.int32)
    f_bias = jnp.linspace(3.0, 6.0, M_HEADS, dtype=f32)
    m_b_if = jnp.concatenate([nrm(ks[22], (N_MLSTM_LAYERS, M_HEADS), 0.1),
                              f_bias[None, :] + nrm(ks[23], (N_MLSTM_LAYERS, M_HEADS), 0.01)], axis=-1)
    return {
        "x_prompt": nrm(ks[0], (BATCH, SEQ, D_MODEL), 1.0),
        "x_sample": nrm(ks[1], (DEC_BATCH, DEC_SEQ, D_MODEL), 1.0),
        "cache_k": nrm(ks[2], (N_ATT_LAYERS, n_pool, PAGE_SIZE, A_HEADS, A_HEAD_DIM), 1.0),
        "cache_v": nrm(ks[3], (N_ATT_LAYERS, n_pool, PAGE_SIZE, A_HEADS, A_HEAD_DIM), 1.0),
        "page_table": page_table,
        "state_C": nrm(ks[5], (N_MLSTM_LAYERS, DEC_BATCH, M_HEADS, M_HEAD_DIM, M_HEAD_DIM), 0.05),
        "state_n": nrm(ks[6], (N_MLSTM_LAYERS, DEC_BATCH, M_HEADS, M_HEAD_DIM), 0.05),
        "state_m": nrm(ks[7], (N_MLSTM_LAYERS, DEC_BATCH, M_HEADS), 1.0),
        "state_conv": nrm(ks[8], (N_MLSTM_LAYERS, DEC_BATCH, CONV_WIDTH - 1, M_WIDTH), 1.0),
        "a_norm": 1.0 + nrm(ks[9], (N_ATT_LAYERS, D_MODEL), 0.02),
        "a_w_in": nrm(ks[10], (N_ATT_LAYERS, D_MODEL, 4 * A_WIDTH), D_MODEL ** -0.5),
        "a_q_norm": 1.0 + nrm(ks[11], (N_ATT_LAYERS, A_HEAD_DIM), 0.02),
        "a_k_norm": 1.0 + nrm(ks[12], (N_ATT_LAYERS, A_HEAD_DIM), 0.02),
        "a_w_out": nrm(ks[13], (N_ATT_LAYERS, A_WIDTH, D_MODEL), A_WIDTH ** -0.5),
        "m_norm": 1.0 + nrm(ks[14], (N_MLSTM_LAYERS, D_MODEL), 0.02),
        "m_w_in": nrm(ks[15], (N_MLSTM_LAYERS, D_MODEL, 3 * M_WIDTH), D_MODEL ** -0.5),
        "m_conv_w": nrm(ks[16], (N_MLSTM_LAYERS, CONV_WIDTH, M_WIDTH), CONV_WIDTH ** -0.5),
        "m_conv_b": nrm(ks[17], (N_MLSTM_LAYERS, M_WIDTH), 0.01),
        "m_w_q": nrm(ks[18], (N_MLSTM_LAYERS, N_QKV_BLOCKS, QKV_BLOCK, QKV_BLOCK), QKV_BLOCK ** -0.5),
        "m_w_k": nrm(ks[19], (N_MLSTM_LAYERS, N_QKV_BLOCKS, QKV_BLOCK, QKV_BLOCK), QKV_BLOCK ** -0.5),
        "m_w_v": nrm(ks[20], (N_MLSTM_LAYERS, N_QKV_BLOCKS, QKV_BLOCK, QKV_BLOCK), QKV_BLOCK ** -0.5),
        "m_w_if": nrm(ks[21], (N_MLSTM_LAYERS, 3 * M_WIDTH, 2 * M_HEADS), (3 * M_WIDTH) ** -0.5),
        "m_b_if": m_b_if,
        "m_out_norm": 1.0 + nrm(ks[24], (N_MLSTM_LAYERS, M_WIDTH), 0.02),
        "m_skip": 1.0 + nrm(ks[25], (N_MLSTM_LAYERS, M_WIDTH), 0.02),
        "m_w_out": nrm(ks[26], (N_MLSTM_LAYERS, M_WIDTH, D_MODEL), M_WIDTH ** -0.5),
    }

def reference(x_prompt, x_sample, cache_k, cache_v, page_table, state_C, state_n, state_m, state_conv,
              a_norm, a_w_in, a_q_norm, a_k_norm, a_w_out,
              m_norm, m_w_in, m_conv_w, m_conv_b, m_w_q, m_w_k, m_w_v, m_w_if, m_b_if,
              m_out_norm, m_skip, m_w_out):
    n_pages = PAST_LEN // PAGE_SIZE
    yp, ys = x_prompt, x_sample
    kp_l, vp_l, ks_l, vs_l = [], [], [], []
    Cp_l, np_l, mp_l, bp_l = [], [], [], []
    Cs_l, ns_l, ms_l, bs_l = [], [], [], []
    for i in range(DEPTH):
        j = i // N_MIXERS
        if i % N_MIXERS == 0:
            wa = (a_norm[j], a_w_in[j], a_q_norm[j], a_k_norm[j], a_w_out[j])
            yp, kp, vp = attention_layer(yp, 0, None, None, *wa)
            k_past = cache_k[j, page_table].reshape(DEC_BATCH, n_pages * PAGE_SIZE, A_HEADS, A_HEAD_DIM)
            v_past = cache_v[j, page_table].reshape(DEC_BATCH, n_pages * PAGE_SIZE, A_HEADS, A_HEAD_DIM)
            ys, ksm, vsm = attention_layer(ys, PAST_LEN, k_past, v_past, *wa)
            kp_l.append(kp); vp_l.append(vp); ks_l.append(ksm); vs_l.append(vsm)
        else:
            wm = (m_norm[j], m_w_in[j], m_conv_w[j], m_conv_b[j], m_w_q[j], m_w_k[j], m_w_v[j],
                  m_w_if[j], m_b_if[j], m_out_norm[j], m_skip[j], m_w_out[j])
            buf0 = jnp.zeros((BATCH, CONV_WIDTH - 1, M_WIDTH), yp.dtype)
            C0 = jnp.zeros((BATCH, M_HEADS, M_HEAD_DIM, M_HEAD_DIM), jnp.float32)
            n0 = jnp.zeros((BATCH, M_HEADS, M_HEAD_DIM), jnp.float32)
            m0 = jnp.zeros((BATCH, M_HEADS), jnp.float32)
            yp, Cp, np_, mp, bp = mlstm_layer(yp, buf0, C0, n0, m0, *wm)
            ys, Cs, ns, ms, bs = mlstm_layer(ys, state_conv[j], state_C[j], state_n[j], state_m[j], *wm)
            Cp_l.append(Cp); np_l.append(np_); mp_l.append(mp); bp_l.append(bp)
            Cs_l.append(Cs); ns_l.append(ns); ms_l.append(ms); bs_l.append(bs)
    return (yp, ys,
            jnp.stack(kp_l), jnp.stack(vp_l), jnp.stack(ks_l), jnp.stack(vs_l),
            jnp.stack(Cp_l), jnp.stack(np_l), jnp.stack(mp_l), jnp.stack(bp_l),
            jnp.stack(Cs_l), jnp.stack(ns_l), jnp.stack(ms_l), jnp.stack(bs_l))


_drawn_inputs = setup_inputs


def setup_inputs(seed=0):
    import zlib

    import numpy as np

    out = dict(_drawn_inputs(seed))
    spreads = {}
    factors = {'a_norm': 2.818, 'a_q_norm': 8.0, 'a_k_norm': 3.068, 'm_out_norm': 5.743, 'm_skip': 8.0}
    for name, (base, spread) in spreads.items():
        noise = np.random.default_rng([zlib.crc32(name.encode()), seed]).standard_normal(out[name].shape)
        drawn = base * np.exp(spread * noise) if base else spread * noise
        out[name] = __import__('jax').numpy.asarray(drawn.astype(out[name].dtype))
    for name, factor in factors.items():
        out[name] = (out[name] * factor).astype(out[name].dtype)
    return out
```

```python
from contextlib import ExitStack

import concourse.bass as bass
from concourse import mybir

F32 = mybir.dt.float32
I32 = mybir.dt.int32
ALU = mybir.AluOpType
ACT = mybir.ActivationFunctionType
AX_X = mybir.AxisListType.X
ds = bass.ds

P = 128
D_MODEL, SEQ, DEC, PAST, PAGE = 1024, 512, 8, 256, 128
TOK = SEQ + DEC
HALF = TOK // 2
EPS = 1e-6
KT = D_MODEL // P
NT = SEQ // P
TT = NT + 1
A_HEADS, A_DIM = 8, 128
A_SCALE = A_DIM ** -0.5
NPG = PAST // PAGE
M_WIDTH, M_HEADS, M_DIM = 2048, 4, 512
MF = M_WIDTH // P
FH = M_DIM // P
K_SCALE = M_DIM ** -0.5
CONV = 4
MASKED = -1.0e30


def rows(t):
    return P if t < NT else DEC


QUADS = [slice(32 * j, 32 * j + DEC) for j in range(4)]
"""Rows of a PSUM bank that sample rows' products take in turn: the array's four column groups work side
by side, and each sums its share of the contraction."""


def need(eng, sem, value):
    if isinstance(value, int) and value <= 0:
        return
    eng.wait_ge(sem, value)


def need_apart(eng, sem, value, tick):
    if not (isinstance(value, int) and value <= 0):
        eng.wait_ge(sem, value)
        eng.sem_inc(tick, 1)


class Chain:

    def __init__(self, eng, sem):
        self.eng, self.sem, self.base, self.n = eng, sem, 0, 0

    def __call__(self, ins):
        self.n += 1
        ins.then_inc(self.sem, 1)
        self.eng.wait_ge(self.sem, self.base + self.n)

    def enter(self, i, per_turn):
        self.outer, self.base, self.n, self.per_turn = self.base + self.n, self.base + self.n + i * per_turn, 0, per_turn

    def leave(self, turns):
        assert self.n == self.per_turn, (self.n, self.per_turn)
        self.base, self.n = self.outer + turns * self.per_turn, 0


class Mem:

    def __init__(self, nc, ctx):
        self.nc, self.ctx, self.sems = nc, ctx, []

    def sb(self, name, shape, dt=F32):
        return self.ctx.enter_context(self.nc.sbuf_tensor(name, shape, dt))

    def ps(self, name, shape):
        return self.ctx.enter_context(self.nc.psum_tensor(name, shape, F32))

    def sem(self, name):
        self.sems.append(self.nc.alloc_semaphore(name=name))
        return self.sems[-1]

    def block(self):
        self.ctx.callback(self.close)
        return self.ctx.enter_context(self.nc.Block())

    def close(self):
        self.nc.clear_and_free_semaphores(self.sems)
        self.nc.all_engine_barrier()


def build_constants(nc, c):
    with ExitStack() as ctx:
        m = Mem(nc, ctx)
        filled, made = m.sem("filled"), m.sem("made")
        block = m.block()

        @block.gpsimd
        def _(pool):
            nc.gpsimd.memset(c.ident[:], 0.0).then_inc(filled, 1)
            nc.gpsimd.memset(c.causal[:], 0.0).then_inc(filled, 1)
            nc.gpsimd.memset(c.minus_half[:], -0.5).then_inc(filled, 1)
            pool.wait_ge(filled, 3)
            nc.gpsimd.affine_select(out=c.ident[:], in_=c.ident[:], compare_op=ALU.not_equal, fill=1.0, base=0,
                                    pattern=[[-1, P]], channel_multiplier=1).then_inc(made, 1)
            nc.gpsimd.affine_select(out=c.causal[:], in_=c.causal[:], compare_op=ALU.is_ge, fill=MASKED, base=0,
                                    pattern=[[-1, P]], channel_multiplier=1).then_inc(made, 1)
            pool.wait_ge(made, 2)


class Norm:

    def __init__(self, nc, m, c, x, hT, gain, x_ready, x_count, tag, gain_ready):
        self.nc, self.c, self.x, self.hT, self.gain = nc, c, x, hT, gain
        self.x_ready, self.x_count, self.gain_ready = x_ready, x_count, gain_ready
        self.xn = m.sb("xn" + tag, [P, 2, D_MODEL])
        self.ss = m.sb("ss" + tag, [P, TT])
        self.r = m.sb("r" + tag, [P, TT])
        self.ps = m.ps("norm_ps" + tag, [P, 2, 512])
        self.sumsq, self.mean, self.rstd, self.scaled, self.turned, self.done = (
            m.sem(n + tag) for n in ("sumsq", "mean", "rstd", "scaled", "turned", "h_ready"))

    def scalar_sums(self, act, t):
        p = rows(t)
        act.wait_ge(self.x_ready[t], self.x_count[t])
        need(act, self.turned, 2 * (t - 1))
        self.nc.scalar.activation(self.xn[0:p, t % 2, :], self.x[0:p, t, :], ACT.Square,
                                  accum_out=self.ss[0:p, t:t + 1]).then_inc(self.sumsq, 1)

    def pool_rstd(self, pool, t):
        p = rows(t)
        pool.wait_ge(self.sumsq, t + 1)
        self.nc.gpsimd.tensor_scalar(self.ss[0:p, t:t + 1], self.ss[0:p, t:t + 1], 1.0 / D_MODEL, EPS,
                                     ALU.mult, ALU.add).then_inc(self.mean, 1)
        pool.wait_ge(self.mean, t + 1)
        self.nc.gpsimd.tensor_tensor(self.r[0:p, t:t + 1], self.ss[0:p, t:t + 1],
                                     self.c.minus_half[0:p, 0:1], ALU.pow).then_inc(self.rstd, 1)

    def vector_scale(self, dve, t):
        p = rows(t)
        dve.wait_ge(self.rstd, t + 1)
        self.nc.vector.tensor_scalar(self.xn[0:p, t % 2, :], self.x[0:p, t, :], self.r[0:p, t:t + 1], None,
                                     ALU.mult).then_inc(self.scaled, 1)

    def vector_store(self, dve, t):
        p = rows(t)
        if t == 0:
            dve.wait_ge(self.gain_ready[0], self.gain_ready[1])
        for g in range(2):
            dve.wait_ge(self.turned, 2 * t + g + 1)
            src = self.ps[:, g, :].rearrange("p (k r) -> p k r", k=4)[:, :, 0:p]
            self.nc.vector.tensor_tensor(self.hT[:, 4 * g:4 * g + 4, t * P:t * P + p], src,
                                         self.gain[:, 4 * g:4 * g + 4].unsqueeze(2).broadcast_to([P, 4, p]),
                                         ALU.mult).then_inc(self.done, 1)

    def tensor_turn(self, pe, t):
        p = rows(t)
        pe.wait_ge(self.scaled, t + 1)
        for g in range(2):
            need(pe, self.done, 2 * t + g - 1)
            for k in range(4):
                last = self.nc.tensor.transpose(self.ps[:, g, k * P:k * P + p],
                                                self.xn[0:p, t % 2, (4 * g + k) * P:(4 * g + k + 1) * P],
                                                self.c.ident[0:p, 0:p])
            last.then_inc(self.turned, 1)


def build_attention(nc, c, io):
    with ExitStack() as ctx:
        m = Mem(nc, ctx)
        x = m.sb("x", [P, TT, D_MODEL])
        hT = c.hT
        gain = m.sb("a_gain", [P, KT])
        w = m.sb("w_in", [P, 2, KT, 4, A_DIM])
        raw = m.sb("raw", [P, 2, TT, 4, A_DIM])
        cos_g = m.sb("cos_g", [P, TT, 2, A_DIM])
        sin_g = m.sb("sin_g", [P, TT, 2, A_DIM])
        rope = m.sb("rope", [P, 2, TT, A_DIM])
        qk_gain = m.sb("qk_gain", [P, 2, A_DIM])
        rot = m.sb("rot", [P, 2, TT, 2, A_DIM])
        qk = m.sb("qk", [P, 2, TT, 2, A_DIM])
        qk_ss = m.sb("qk_ss", [P, 2, TT, 2])
        th = m.sb("th", [P, TT, A_DIM])
        sg = m.sb("sg", [P, 2, TT, A_DIM])
        qT, kT, gT = (m.sb(n, [P, SEQ]) for n in ("qT", "kT", "gT"))
        prob = m.sb("prob", [P, NT, SEQ])
        probT = m.sb("probT", [P, NT, SEQ])
        nmax, rsum, rinv = (m.sb(n, [P, NT]) for n in ("nmax", "rsum", "rinv"))
        nm = Norm(nc, m, c, x, hT, gain, x_ready := [m.sem(f"x_ready{t}") for t in range(TT)], [16] * TT, "_a", (in_ready := m.sem("in_ready"), 16 * 5))
        pj = m.ps("pj", [P, 2, 512])
        tr = nm.ps
        sc = m.ps("sc", [P, 2, 512])
        ops = m.ps("o_ps", [P, 512])

        (w_loaded0, w_loaded1, w_used, proj, raw_ready, tanh_ready, ss_ready, mean_ready, rstd_ready, qk_ready,
         sg_ready, tr_ready, tr_taken, s_ready, nmax_ready, p_exp, p_normed, o_ready, o_gated,
         smp_taken, tables_ready, dve_step, zeroed, pool_tick, smp_summed) = (m.sem(n) for n in (
             "w_loaded0", "w_loaded1", "w_used", "proj", "raw_ready", "tanh_ready", "qk_ss_ready", "qk_mean_ready",
             "qk_rstd_ready", "qk_ready", "sg_ready", "tr_ready", "tr_taken", "s_ready", "nmax_ready", "p_exp",
             "p_normed", "o_ready", "o_gated", "smp_taken", "tables_ready", "dve_step",
             "zeroed", "pool_tick", "smp_summed"))
        w_loaded = (w_loaded0, w_loaded1)
        k_stored, v_stored = ([m.sem(f"{n}_stored{j}") for j in range(2)] for n in "kv")
        smp_stored = m.sem("smp_stored")
        w_view = io.a_w_in.rearrange("(k p) (m n) -> p k m n", p=P, m=4)
        block = m.block()

        @block.sync
        def _(sp):
            for t in range(NT):
                sp.dma_start(x[:, t, :], io.x_prompt[t * P:(t + 1) * P, :]).then_inc(x_ready[t], 16)
            sp.dma_start(x[0:DEC, NT, :], io.x_sample).then_inc(x_ready[NT], 16)

            def load_w(h, j):
                need(sp, w_used, h - 1)
                for q in range(4):
                    sp.dma_start(w[:, j, :, q, :], w_view[:, :, q, ds(h * A_DIM, A_DIM)]).then_inc(w_loaded[j], 16)

            def store_kv(h, j):
                sp.wait_ge(qk_ready, h + 1)
                sp.dma_start(io.k_prompt.rearrange("(t p) n -> p t n", p=P)[:, :, ds(h * A_DIM, A_DIM)],
                             qk[:, j, 0:NT, 1, :]).then_inc(k_stored[j], 16)
                sp.dma_start(io.v_prompt.rearrange("(t p) n -> p t n", p=P)[:, :, ds(h * A_DIM, A_DIM)],
                             raw[:, j, 0:NT, 2, :]).then_inc(v_stored[j], 16)

            load_w(0, 0)
            load_w(1, 1)
            with sp.Fori(0, A_HEADS // 2 - 1) as i:
                for j in range(2):
                    load_w(2 * i + 2 + j, j)
                    store_kv(2 * i + j, j)
            for h in (A_HEADS - 2, A_HEADS - 1):
                store_kv(h, h % 2)
            sp.wait_ge(smp_taken, A_HEADS)
            sp.dma_start(io.k_sample, c.smp[:, 1, :]).then_inc(smp_stored, 16)
            sp.dma_start(io.v_sample, c.smp[:, 2, :]).then_inc(smp_stored, 16)
            sp.dma_start(io.q_rows, c.smp[:, 0, :]).then_inc(smp_stored, 16)
            sp.wait_ge(smp_stored, 16 * 3)
            for j in range(2):
                sp.wait_ge(k_stored[j], 16 * A_HEADS // 2)
                sp.wait_ge(v_stored[j], 16 * A_HEADS // 2)

        @block.scalar
        def _(act):
            act.dma_start(gain[:], io.a_norm.rearrange("(k p) -> p k", p=P)).then_inc(in_ready, 16)
            for s in range(2):
                act.dma_start(rope[:, s], io.rope[s].rearrange("(t p) d -> p t d", p=P)).then_inc(in_ready, 16)
            act.dma_start(qk_gain[:, 0, :], io.a_q_norm.partition_broadcast(P)).then_inc(in_ready, 16)
            act.dma_start(qk_gain[:, 1, :], io.a_k_norm.partition_broadcast(P)).then_inc(in_ready, 16)
            for t in range(TT):
                nm.scalar_sums(act, t)

            def take_proj(h, j, t, turn):
                p = rows(t)
                if t == 0:
                    need(act, o_ready, h - 1)
                    need(act, v_stored[j], 16 * turn)
                    need(act, smp_taken, h - 1)
                act.wait_ge(proj, TT * h + t + 1)
                nc.scalar.copy(raw[0:p, j, t, :, :].rearrange("p m d -> p (m d)"),
                               pj[0:p, (TT * j + t) % 2, :]).then_inc(raw_ready, 1)

            def tanh(h, j):
                act.wait_ge(raw_ready, TT * (h + 1))
                act.wait_ge(smp_summed, h + 1)
                need(act, sg_ready, h)
                nc.scalar.activation(th[:], raw[:, j, :, 3, :], ACT.Tanh, scale=0.5).then_inc(tanh_ready, 1)

            def take_tr(h, j, g):
                act.wait_ge(tr_ready, 7 * h + g + 1)
                src = tr[:, (7 * j + g) % 2, :]
                if g < 2:
                    need(act, s_ready, NT * h)
                    nc.scalar.copy((qT, kT)[g][:], src).then_inc(tr_taken, 1)
                elif g == 2:
                    need(act, o_gated, h)
                    nc.scalar.copy(gT[:], src).then_inc(tr_taken, 1)
                else:
                    t = g - 3
                    need(act, o_ready, h)
                    nc.scalar.copy(probT[:, 0:t + 1, t * P:(t + 1) * P],
                                   src[:, 0:(t + 1) * P].rearrange("p (k q) -> p k q", q=P)).then_inc(tr_taken, 1)

            def exp(h, j, t):
                act.wait_ge(nmax_ready, NT * h + t + 1)
                need(act, tr_ready, 7 * (h - 1) + 4 + t)
                nc.scalar.activation(prob[:, t, 0:(t + 1) * P], sc[:, t % 2, 0:(t + 1) * P], ACT.Exp,
                                     bias=nmax[:, t:t + 1], scale=A_SCALE,
                                     accum_out=rsum[:, t:t + 1]).then_inc(p_exp, 1)

            def step(h, j, turn=0, with_next=True):
                n = (lambda t: take_proj(h + 1, 1 - j, t, turn)) if with_next else (lambda t: None)
                n(0)
                n(1)
                for g in range(3):
                    take_tr(h, j, g)
                n(2)
                exp(h, j, 0)
                exp(h, j, 1)
                n(3)
                exp(h, j, 2)
                exp(h, j, 3)
                take_tr(h, j, 3)
                take_tr(h, j, 4)
                n(4)
                take_tr(h, j, 5)
                take_tr(h, j, 6)
                if with_next:
                    tanh(h + 1, 1 - j)

            act.wait_ge(zeroed, 1)
            for t in range(TT):
                take_proj(0, 0, t, 0)
            tanh(0, 0)
            step(0, 0)
            with act.Fori(0, A_HEADS // 2 - 1) as i:
                step(2 * i + 1, 1, i + 1)
                step(2 * i + 2, 0, i + 1)
            step(A_HEADS - 1, 1, with_next=False)

        @block.gpsimd
        def _(pool):
            nc.gpsimd.memset(raw[:, :, NT, :, :], 0.0).then_inc(zeroed, 1)
            for t in range(TT):
                nm.pool_rstd(pool, t)

            def head(h, j):
                pool.wait_ge(mean_ready, h + 1)
                nc.gpsimd.tensor_tensor(qk_ss[:, j], qk_ss[:, j], c.minus_half[:, 0:2 * TT].rearrange("p (t m) -> p t m", m=2),
                                        ALU.pow).then_inc(rstd_ready, 1)
                need_apart(pool, qk_ready, h + 1, pool_tick)
                need_apart(pool, sg_ready, h + 1, pool_tick)
                nc.gpsimd.tensor_copy(c.smp[:, 0:2, ds(h * A_DIM, A_DIM)], qk[0:DEC, j, NT, :, :])
                nc.gpsimd.tensor_copy(c.smp[:, 2, ds(h * A_DIM, A_DIM)], raw[0:DEC, j, NT, 2, :])
                nc.gpsimd.tensor_copy(c.smp[:, 3, ds(h * A_DIM, A_DIM)], sg[0:DEC, j, NT, :]).then_inc(smp_taken, 1)

            with pool.Fori(0, A_HEADS // 2) as i:
                head(2 * i, 0)
                head(2 * i + 1, 1)

        @block.vector
        def _(dve):
            chain = Chain(dve, dve_step)
            nm.vector_scale(dve, 0)
            for t in range(TT):
                if t + 1 < TT:
                    nm.vector_scale(dve, t + 1)
                nm.vector_store(dve, t)
            half = A_DIM // 2
            for q in range(2):
                g = qk_gain[:, q:q + 1, :].broadcast_to([P, TT, A_DIM])
                nc.vector.tensor_tensor(cos_g[:, :, q, :], rope[:, 0], g, ALU.mult)
                nc.vector.tensor_tensor(sin_g[:, :, q, 0:half], rope[:, 1, :, 0:half], g[:, :, half:], ALU.mult)
                last = nc.vector.tensor_tensor(sin_g[:, :, q, half:], rope[:, 1, :, half:], g[:, :, 0:half], ALU.mult)
            chain(last)

            def norm_rope(h, j, turn):
                dve.wait_ge(raw_ready, TT * (h + 1))
                smp, bank = raw[0:DEC, j, NT, :, :].rearrange("p m d -> p (m d)"), pj[:, (TT * j + NT) % 2, :]
                chain(nc.vector.tensor_tensor(smp, smp, bank[QUADS[1], :], ALU.add))
                chain(nc.vector.tensor_tensor(smp, smp, bank[QUADS[2], :], ALU.add))
                nc.vector.tensor_tensor(smp, smp, bank[QUADS[3], :], ALU.add).then_inc(smp_summed, 1)
                dve.wait_ge(smp_summed, h + 1)
                src = raw[:, j, :, 0:2, :]
                chain(nc.vector.tensor_tensor(rot[:, 0], src, src, ALU.mult))
                need(dve, smp_taken, h - 1)
                nc.vector.tensor_reduce(qk_ss[:, j], rot[:, 0], AX_X, ALU.add).then_inc(ss_ready, 1)
                dve.wait_ge(ss_ready, h + 1)
                nc.vector.tensor_scalar(qk_ss[:, j], qk_ss[:, j], 1.0 / A_DIM, EPS, ALU.mult,
                                        ALU.add).then_inc(mean_ready, 1)
                nc.vector.tensor_tensor(rot[:, 0, :, :, :], src, cos_g[:], ALU.mult)
                nc.vector.tensor_tensor(rot[:, 1, :, :, 0:half], src[:, :, :, half:], sin_g[:, :, :, 0:half], ALU.mult)
                chain(nc.vector.tensor_tensor(rot[:, 1, :, :, half:], src[:, :, :, 0:half], sin_g[:, :, :, half:],
                                              ALU.mult))
                chain(nc.vector.tensor_tensor(rot[:, 0], rot[:, 0], rot[:, 1], ALU.add))
                dve.wait_ge(rstd_ready, h + 1)
                need(dve, tr_ready, 7 * (h - 1))
                need(dve, k_stored[j], 16 * turn)
                nc.vector.tensor_tensor(qk[:, j], rot[:, 0], qk_ss[:, j].unsqueeze(3).broadcast_to([P, TT, 2, A_DIM]),
                                        ALU.mult).then_inc(qk_ready, 1)
                dve.wait_ge(qk_ready, h + 1)
                dve.wait_ge(tanh_ready, h + 1)
                nc.vector.scalar_tensor_tensor(out=sg[:, j], in0=th[:], scalar=1.0, in1=raw[:, j, :, 3, :],
                                               op0=ALU.add, op1=ALU.mult).then_inc(sg_ready, 1)

            def softmax(h, t):
                dve.wait_ge(s_ready, NT * h + t + 1)
                d = sc[:, t % 2, t * P:(t + 1) * P]
                chain(nc.vector.tensor_tensor(d, d, c.causal[:], ALU.add))
                chain(nc.vector.tensor_reduce(nmax[:, t:t + 1], sc[:, t % 2, 0:(t + 1) * P], AX_X, ALU.max, negate=True))
                nc.vector.tensor_scalar(nmax[:, t:t + 1], nmax[:, t:t + 1], A_SCALE, None,
                                        ALU.mult).then_inc(nmax_ready, 1)

            def norm_probs(h, t):
                dve.wait_ge(p_exp, NT * h + t + 1)
                chain(nc.vector.reciprocal(rinv[:, t:t + 1], rsum[:, t:t + 1]))
                nc.vector.tensor_scalar(prob[:, t, 0:(t + 1) * P], prob[:, t, 0:(t + 1) * P], rinv[:, t:t + 1], 0.5,
                                        ALU.mult, ALU.mult).then_inc(p_normed, 1)

            def head(h, j, turn):
                norm_rope(h, j, turn)
                for t in range(NT):
                    softmax(h, t)
                    if t:
                        norm_probs(h, t - 1)
                norm_probs(h, NT - 1)
                dve.wait_ge(o_ready, h + 1)
                dve.wait_ge(tr_taken, 7 * h + 3)
                nc.vector.tensor_tensor(c.oT[:, ds(h, 1), 0:SEQ].rearrange("p a q -> p (a q)"), ops[:], gT[:],
                                        ALU.mult).then_inc(o_gated, 1)

            head(0, 0, 0)
            head(1, 1, 0)
            with dve.Fori(0, A_HEADS // 2 - 1) as i:
                chain.enter(i, 2 * 17)
                head(2 * i + 2, 0, i + 1)
                head(2 * i + 3, 1, i + 1)
                chain.leave(A_HEADS // 2 - 1)

        @block.tensor
        def _(pe):
            for t in range(TT):
                nm.tensor_turn(pe, t)

            def project(h, j, t, turn):
                if t == 0:
                    pe.wait_ge(w_loaded[j], 64 * (turn + 1))
                p = rows(t)
                need(pe, raw_ready, TT * h + t - 1)
                if t == 1:
                    need(pe, smp_summed, h)
                for k in range(KT):
                    out = slice(0, P) if t < NT else QUADS[k % 4]
                    sums = 1 if t < NT else 4
                    last = nc.tensor.matmul(pj[out, (TT * j + t) % 2, :], hT[:, k, t * P:t * P + p],
                                            w[:, j, k, :, :].rearrange("p m d -> p (m d)"),
                                            start=(k < sums), stop=(k >= KT - sums))
                last.then_inc(proj, 1)
                if t == TT - 1:
                    pe.wait_ge(proj, TT * (h + 1))
                    pe.sem_inc(w_used, 1)

            def turn_group(h, j, g):
                need(pe, tr_taken, 7 * h + g - 1)
                bank = tr[:, (7 * j + g) % 2, :]
                if g < 3:
                    if g == 0:
                        pe.wait_ge(sg_ready, h + 1)
                    for t in range(NT):
                        src = sg[:, j, t, :] if g == 2 else qk[:, j, t, g, :]
                        last = nc.tensor.transpose(bank[:, t * P:(t + 1) * P], src, c.ident[:])
                else:
                    t = g - 3
                    pe.wait_ge(p_normed, NT * h + t + 1)
                    for k in range(t + 1):
                        last = nc.tensor.transpose(bank[:, k * P:(k + 1) * P], prob[:, t, k * P:(k + 1) * P], c.ident[:])
                last.then_inc(tr_ready, 1)

            def scores(h, t):
                if t == 0:
                    pe.wait_ge(tr_taken, 7 * h + 2)
                need(pe, p_exp, NT * h + t - 1)
                nc.tensor.matmul(sc[:, t % 2, 0:(t + 1) * P], qT[:, t * P:(t + 1) * P], kT[:, 0:(t + 1) * P],
                                 start=True, stop=True).then_inc(s_ready, 1)

            def values(h, j):
                pe.wait_ge(tr_taken, 7 * h + 7)
                need(pe, o_gated, h)
                for k in range(NT):
                    last = nc.tensor.matmul(ops[:, k * P:], raw[:, j, k, 2, :], probT[:, k, k * P:],
                                            start=(k == 0), stop=(k == NT - 1))
                last.then_inc(o_ready, 1)

            def step(h, j, turn, with_next=True):
                n = (lambda t: project(h + 1, 1 - j, t, turn)) if with_next else (lambda t: None)
                n(0)
                n(1)
                for g in range(3):
                    turn_group(h, j, g)
                n(2)
                scores(h, 0)
                scores(h, 1)
                n(3)
                scores(h, 2)
                scores(h, 3)
                turn_group(h, j, 3)
                turn_group(h, j, 4)
                n(4)
                turn_group(h, j, 5)
                turn_group(h, j, 6)
                values(h, j)

            pe.wait_ge(nm.done, 2 * TT)
            for t in range(TT):
                project(0, 0, t, 0)
            step(0, 0, 0)
            with pe.Fori(0, A_HEADS // 2 - 1) as i:
                step(2 * i + 1, 1, i + 1)
                step(2 * i + 2, 0, i + 1)
            step(A_HEADS - 1, 1, 0, with_next=False)


def build_sample_attention_and_out(nc, c, io):
    N_ROW = DEC * A_HEADS
    with ExitStack() as ctx:
        m = Mem(nc, ctx)
        x = m.sb("x_b", [P, TT, D_MODEL])
        wo = m.sb("w_out_a", [P, A_HEADS, D_MODEL])
        gain = m.sb("m_gain", [P, KT])
        pages = m.sb("pages", [1, DEC * NPG], I32)
        kc = m.sb("k_cache", [P, 2, NPG, D_MODEL])
        vc = m.sb("v_cache", [P, 2, NPG, D_MODEL])
        qb = m.sb("q_bcast", [P, 2, D_MODEL])
        score = m.sb("score", [P, NPG, DEC, A_HEADS])
        own_prod = m.sb("own_prod", [DEC, D_MODEL])
        own = m.sb("own", [DEC, A_HEADS])
        own_col = m.sb("own_col", [N_ROW, 1])
        prob = m.sb("prob_b", [N_ROW, PAST])
        own_p = m.sb("own_p", [N_ROW, 1])
        nmax, rsum, rinv = (m.sb(n + "_b", [N_ROW, 1]) for n in ("nmax", "rsum", "rinv"))
        probT = m.sb("probT_b", [P, NPG, DEC, A_HEADS])
        pick = m.sb("pick", [P, DEC, DEC])
        p_at = m.sb("p_at", [P, 2, NPG, A_HEADS, DEC])
        o_s = m.sb("o_s", [DEC, D_MODEL])
        zero = m.sb("zero_b", [P, DEC])
        taken = m.sem("x1_taken")
        nm = Norm(nc, m, c, x, c.hT, gain, [taken] * TT, [2 * (t + 1) for t in range(TT)], "_b",
                  (gain_in := m.sem("gain_in"), 16))
        out_ps = m.ps("out_ps", [P, 2, 512])
        sp_ps = m.ps("sp_ps", [P, 2, 512])
        o_ps = m.ps("os_ps", [P, 512])
        (x_in, wo_in, pages_in, v_in0, v_in1, k_in0, k_in1, score_done, out_done, own_kept, own_back,
         sc_turned, max_ready, p_exp, p_normed, p_turned, p_taken, at_ready, v_used, os_ready, os_gated, os_turned,
         os_taken, own_pk, own_pb, x1_stored, step, picked, zeroed) = (m.sem(n + "_b") for n in (
             "x_in", "wo_in", "pages_in", "v_in0", "v_in1", "k_in0", "k_in1", "score_done", "out_done",
             "own_kept", "own_back", "sc_turned", "max_ready", "p_exp", "p_normed", "p_turned", "p_taken",
             "at_ready", "v_used", "os_ready", "os_gated", "os_turned", "os_taken", "own_pk", "own_pb", "x1_stored",
             "step", "picked", "zeroed"))
        k_in, v_in = (k_in0, k_in1), (v_in0, v_in1)
        n_pool = io.cache_k.shape[0]
        block = m.block()

        @block.sync
        def _(sp):
            sp.dma_start(pages[:], io.page_table).then_inc(pages_in, 16)
            sp.wait_ge(pages_in, 16)

            def load(cache, dst, b, sem):
                for g in range(NPG):
                    page = sp.value_load(pages[0:1, NPG * b + g:NPG * b + g + 1], min_val=0, max_val=n_pool - 1)
                    sp.dma_start(dst[:, b % 2, g, :], cache[ds(page, 1), :, :].rearrange("a p n -> (a p) n")).then_inc(sem, 16)

            def load_k(b):
                if b >= 2:
                    sp.wait_ge(score_done, b - 1)
                load(io.cache_k, kc, b, k_in[b % 2])
                sp.dma_start(qb[:, b % 2, :], io.q_rows[b, :].partition_broadcast(P)).then_inc(k_in[b % 2], 16)

            def load_v(b):
                if b >= 2:
                    sp.wait_ge(v_used, b - 1)
                load(io.cache_v, vc, b, v_in[b % 2])

            load_k(0)
            load_k(1)
            load_v(0)
            load_v(1)
            for b in range(2, DEC):
                load_k(b)
            for t in range(NT):
                sp.wait_ge(taken, 2 * (t + 1))
                sp.dma_start(io.x1_p[t * P:(t + 1) * P, :], x[:, t, :]).then_inc(x1_stored, 16)
            sp.wait_ge(p_normed, 2)
            sp.dma_start(io.own_cells, own_p[:]).then_inc(own_pk, 16)
            sp.wait_ge(own_pk, 16)
            sp.dma_start(own[:], io.own_cells.rearrange("(b h) a -> b (h a)", b=DEC)).then_inc(own_pb, 16)
            for b in range(2, DEC):
                load_v(b)
            sp.wait_ge(taken, 2 * TT)
            sp.dma_start(io.x1_s, x[0:DEC, NT, :]).then_inc(x1_stored, 16)
            sp.wait_ge(x1_stored, 16 * TT)

        @block.scalar
        def _(act):
            act.dma_start(wo[:], io.a_w_out.rearrange("(h p) n -> p h n", p=P)).then_inc(wo_in, 16)
            act.dma_start(x[:, 0:NT, :], io.x_prompt.rearrange("(t p) n -> p t n", p=P)).then_inc(x_in, 16)
            act.dma_start(x[0:DEC, NT, :], io.x_sample).then_inc(x_in, 16)
            act.dma_start(gain[:], io.m_norm.rearrange("(k p) -> p k", p=P)).then_inc(gain_in, 16)
            act.wait_ge(own_kept, 1)
            act.dma_start(io.own_scores, own[:]).then_inc(own_back, 16)
            act.wait_ge(own_back, 16)
            act.dma_start(own_col[:], io.own_scores.rearrange("b (h a) -> (b h) a", a=1)).then_inc(own_back, 16)
            nm.scalar_sums(act, 0)
            nm.scalar_sums(act, 1)
            act.wait_ge(max_ready, 1)
            nc.scalar.activation(prob[:], sp_ps[0:N_ROW, 0, 0:PAST], ACT.Exp, bias=nmax[:], scale=A_SCALE,
                                 accum_out=rsum[:]).then_inc(p_exp, 1)
            nc.scalar.activation(own_p[:], own_col[:], ACT.Exp, bias=nmax[:], scale=A_SCALE).then_inc(p_exp, 1)
            for t in range(2, TT):
                nm.scalar_sums(act, t)

        @block.gpsimd
        def _(pool):
            nc.gpsimd.memset(pick[:], 0.0).then_inc(zeroed, 1)
            nc.gpsimd.memset(zero[:], 0.0).then_inc(zeroed, 1)
            pool.wait_ge(zeroed, 2)
            nc.gpsimd.affine_select(out=pick[:], in_=pick[:], compare_op=ALU.not_equal, fill=1.0, base=0,
                                    pattern=[[1, DEC], [-1, DEC]], channel_multiplier=0).then_inc(picked, 1)
            for t in range(TT):
                nm.pool_rstd(pool, t)

        @block.vector
        def _(dve):
            chain = Chain(dve, step)

            def by_head(a):
                return a.rearrange("p (h d) -> p h d", h=A_HEADS)

            def score_of(b):
                dve.wait_ge(k_in[b % 2], 48 * (b // 2 + 1))
                k = kc[:, b % 2]
                chain(nc.vector.tensor_tensor(k, k, qb[:, b % 2:b % 2 + 1, :].broadcast_to([P, NPG, D_MODEL]), ALU.mult))
                nc.vector.tensor_reduce(score[:, :, b, :], k.rearrange("p g (h d) -> p g h d", h=A_HEADS), AX_X,
                                        ALU.add).then_inc(score_done, 1)

            def take(g):
                t, n = divmod(g, 2)
                p = rows(t)
                dve.wait_ge(out_done, g + 1)
                cols = x[0:p, t, n * 512:(n + 1) * 512]
                if t == NT:
                    for j in (1, 2, 3):
                        chain(nc.vector.tensor_tensor(cols, cols, out_ps[QUADS[j], g % 2, :], ALU.add))
                nc.vector.tensor_tensor(cols, cols, out_ps[0:p, g % 2, :], ALU.add).then_inc(taken, 1)

            chain(nc.vector.tensor_tensor(own_prod[:], c.smp[:, 0, :], c.smp[:, 1, :], ALU.mult))
            nc.vector.tensor_reduce(own[:], by_head(own_prod[:]), AX_X, ALU.add).then_inc(own_kept, 1)
            dve.wait_ge(x_in, 32)
            for b in range(DEC):
                score_of(b)
                take(b)
            dve.wait_ge(sc_turned, 1)
            chain(nc.vector.tensor_reduce(nmax[:], sp_ps[0:N_ROW, 0, 0:PAST], AX_X, ALU.max))
            dve.wait_ge(own_back, 32)
            nc.vector.tensor_scalar(nmax[:], nmax[:], own_col[:, 0:1], -A_SCALE, ALU.max,
                                    ALU.mult).then_inc(max_ready, 1)
            nm.vector_scale(dve, 0)
            nm.vector_scale(dve, 1)
            nm.vector_store(dve, 0)
            dve.wait_ge(p_exp, 2)
            chain(nc.vector.tensor_tensor(rsum[:], rsum[:], own_p[:], ALU.add))
            chain(nc.vector.reciprocal(rinv[:], rsum[:]))
            nc.vector.tensor_scalar(prob[:], prob[:], rinv[:, 0:1], None, ALU.mult).then_inc(p_normed, 1)
            nc.vector.tensor_scalar(own_p[:], own_p[:], rinv[:, 0:1], None, ALU.mult).then_inc(p_normed, 1)
            nm.vector_scale(dve, 2)
            nm.vector_store(dve, 1)
            nm.vector_scale(dve, 3)
            dve.wait_ge(p_turned, 1)
            nc.vector.tensor_copy(probT[:].rearrange("p g b h -> p g (b h)"),
                                  sp_ps[:, 1, 0:NPG * N_ROW].rearrange("p (g r) -> p g r", g=NPG)).then_inc(p_taken, 1)
            dve.wait_ge(p_taken, 1)
            dve.wait_ge(picked, 1)

            def place(b):
                if b >= 2:
                    dve.wait_ge(v_used, b - 1)
                nc.vector.tensor_tensor(p_at[:, b % 2], probT[:, :, b, :].unsqueeze(3).broadcast_to([P, NPG, A_HEADS, DEC]),
                                        pick[:, b, :].unsqueeze(1).unsqueeze(1).broadcast_to([P, NPG, A_HEADS, DEC]),
                                        ALU.mult).then_inc(at_ready, 1)

            place(0)
            place(1)
            nm.vector_store(dve, 2)
            nm.vector_store(dve, 3)
            for b in range(2, DEC):
                place(b)
            dve.wait_ge(own_pb, 16)
            chain(nc.vector.tensor_tensor(by_head(own_prod[:]), by_head(c.smp[:, 2, :]),
                                          own[:].unsqueeze(2).broadcast_to([DEC, A_HEADS, A_DIM]), ALU.mult))
            dve.wait_ge(os_ready, 1)
            by_quad = own_prod[:].rearrange("p (n j d) -> p n j d", n=2, j=4)
            for j in range(4):
                last = nc.vector.tensor_tensor(by_quad[:, :, j, :], by_quad[:, :, j, :],
                                               o_ps[QUADS[j], 0:2 * A_DIM].rearrange("p (n d) -> p n d", n=2), ALU.add)
            chain(last)
            nc.vector.scalar_tensor_tensor(out=o_s[:], in0=own_prod[:], scalar=0.5, in1=c.smp[:, 3, :],
                                           op0=ALU.mult, op1=ALU.mult).then_inc(os_gated, 1)
            dve.wait_ge(os_turned, 1)
            nc.vector.tensor_copy(c.oT[:, :, SEQ:TOK],
                                  sp_ps[:, 0, 0:N_ROW].rearrange("p (h b) -> p h b", h=A_HEADS)).then_inc(os_taken, 1)
            take(2 * NT)
            take(2 * NT + 1)
            nm.vector_scale(dve, NT)
            nm.vector_store(dve, NT)

        @block.tensor
        def _(pe):
            def out_group(g):
                t, n = divmod(g, 2)
                p = rows(t)
                if g >= 2:
                    pe.wait_ge(taken, g - 1)
                for h in range(A_HEADS):
                    out, sums = (slice(0, P), 1) if t < NT else (QUADS[h % 4], 4)
                    last = nc.tensor.matmul(out_ps[out, g % 2, :], c.oT[:, h, t * P:t * P + p],
                                            wo[:, h, n * 512:(n + 1) * 512], start=(h < sums), stop=(h >= A_HEADS - sums))
                last.then_inc(out_done, 1)

            pe.wait_ge(wo_in, 16)
            for g in range(2 * NT - 1):
                out_group(g)
            pe.wait_ge(score_done, DEC)
            for g in range(NPG):
                last = nc.tensor.transpose(sp_ps[0:N_ROW, 0, g * P:(g + 1) * P],
                                           score[:, g].rearrange("p b h -> p (b h)"), c.ident[:])
            last.then_inc(sc_turned, 1)
            out_group(2 * NT - 1)
            nm.tensor_turn(pe, 0)
            nm.tensor_turn(pe, 1)
            pe.wait_ge(p_normed, 1)
            for g in range(NPG):
                last = nc.tensor.transpose(sp_ps[:, 1, g * N_ROW:(g + 1) * N_ROW], prob[:, g * P:(g + 1) * P],
                                           c.ident[0:N_ROW, 0:N_ROW])
            last.then_inc(p_turned, 1)
            nm.tensor_turn(pe, 2)
            nm.tensor_turn(pe, 3)
            pe.wait_ge(zeroed, 2)
            for j in range(4):
                nc.tensor.matmul(o_ps[QUADS[j], :], zero[:], wo[:, 0, 0:512], start=True, stop=True)
            with pe.Fori(0, DEC // 2) as i:
                for j in range(2):
                    pe.wait_ge(v_in[j], 32 * i + 32)
                    pe.wait_ge(at_ready, 2 * i + j + 1)
                    for g in range(NPG):
                        for h in range(A_HEADS):
                            cols = o_ps[QUADS[h % 4], (h // 4) * A_DIM:(h // 4 + 1) * A_DIM]
                            last = nc.tensor.matmul(cols, p_at[:, j, g, h, :], vc[:, j, g, h * A_DIM:(h + 1) * A_DIM],
                                                    start=False, stop=True, skip_group_check=True)
                    last.then_inc(v_used, 1)
            pe.wait_ge(v_used, DEC)
            pe.sem_inc(os_ready, 1)
            pe.wait_ge(os_gated, 1)
            for h in range(A_HEADS):
                last = nc.tensor.transpose(sp_ps[:, 0, h * DEC:(h + 1) * DEC], o_s[:, h * A_DIM:(h + 1) * A_DIM],
                                           c.ident[0:DEC, 0:DEC])
            last.then_inc(os_turned, 1)
            pe.wait_ge(os_taken, 1)
            out_group(2 * NT)
            out_group(2 * NT + 1)
            nm.tensor_turn(pe, NT)


def build_conv_and_gates(nc, c, io):
    N_VEC = CONV * MF + 3 * MF
    PAD = CONV - 1
    S0 = PAD + SEQ
    with ExitStack() as ctx:
        m = Mem(nc, ctx)
        w = m.sb("w_xm", [P, 2, KT, 2 * P])
        vec = m.sb("vec_rows", [N_VEC, P])
        st_rows = m.sb("st_rows", [DEC * PAD, M_WIDTH])
        st = m.sb("st", [P, MF, DEC, PAD])
        w_if = m.sb("w_if", [P, 3, MF, 4, 2 * M_HEADS])
        w_fold = m.sb("w_fold", [P, 3, MF, 4, 2 * M_HEADS])
        w_eff = m.sb("w_eff", [P, 2, MF, 2 * M_HEADS])
        w_eff2 = m.sb("w_eff2", [P, 3, MF, 2 * M_HEADS])
        w_now = m.sb("w_now", [P, 2, FH, 2 * M_HEADS])
        xm = m.sb("xm", [P, FH, PAD + TOK])
        xc = m.sb("xc", [P, FH, TOK])
        u = m.sb("conv_half", [P, FH, TOK])
        th = m.sb("th_c", [P, 2, TOK])
        last_rows = m.sb("last_rows", [PAD + DEC, M_DIM])
        zero = m.sb("zero_c", [P, 2 * M_HEADS])
        bias = m.sb("gate_bias", [2 * M_HEADS, 1])
        gate = m.sb("gate", [2 * M_HEADS, TOK])
        fg, na, lf, ones, b_sum, m_run, bm, ib = (m.sb(n, [M_HEADS, TOK]) for n in (
            "fg", "na", "logf", "ones", "b_sum", "m_run", "bm", "ib"))
        m0 = m.sb("m0", [M_HEADS, DEC])
        inter = m.sb("inter", [M_HEADS, DEC])
        steps = m.sb("steps", [M_HEADS, 3, DEC])
        xm_ps = m.ps("xm_ps", [P, 4, 512])
        gate_ps = m.ps("gate_ps", [P, 512])
        row_ps = m.ps("row_ps", [P, 512])
        prep_ps = m.ps("prep_ps", [P, 512])
        (w_in0, w_in1, w_used, vec_in, st_in, w_if_in, small_in, vec_turned, st_turned, vec_ready, st_ready,
         step, proj, xm_ready, conv_ready, tanh_ready, xc_ready, gates_done, rows_turned, rows_taken, rows_stored,
         xm_kept, xc_kept, eff_ready, now_ready, zeroed, gate_ready, f_moved, exp_ready, m_ready, steps_ready,
         row_out, carried, tick, blk_in) = (m.sem(n + "_c") for n in (
             "w_in0", "w_in1", "w_used", "vec_in", "st_in", "w_if_in", "small_in", "vec_turned", "st_turned",
             "vec_ready", "st_ready", "step", "proj", "xm_ready", "conv_ready", "tanh_ready", "xc_ready", "gates_done",
             "rows_turned", "rows_taken", "rows_stored", "xm_kept", "xc_kept", "eff_ready", "now_ready", "zeroed",
             "gate_ready", "f_moved", "exp_ready", "m_ready", "steps_ready", "row_out", "carried", "tick", "blk_in"))
        w_in = (w_in0, w_in1)
        w_view = io.m_w_in.rearrange("(k p) n -> p k n", p=P)
        PREP = 3 + 3 * 4 + 3
        block = m.block()

        @block.sync
        def _(sp):
            def load_w(h):
                for s in range(2):
                    need(sp, w_used, 2 * h + s - 1)
                    sp.dma_start(w[:, s], w_view[:, :, ds(h * M_DIM + s * 2 * P, 2 * P)]).then_inc(w_in[s], 16)

            load_w(0)
            sp.dma_start(vec[0:CONV * MF, :], io.m_conv_w.rearrange("j (f p) -> (j f) p", p=P)).then_inc(vec_in, 16)
            for n, v in enumerate((io.m_conv_b, io.m_out_norm, io.m_skip)):
                sp.dma_start(vec[(CONV + n) * MF:(CONV + n + 1) * MF, :], v.rearrange("(f p) -> f p", p=P)).then_inc(vec_in, 16)
            sp.dma_start(st_rows[:], io.state_conv.rearrange("b j n -> (b j) n")).then_inc(st_in, 16)
            sp.dma_start(bias[:], io.m_b_if.rearrange("(n a) -> n a", a=1)).then_inc(small_in, 16)
            sp.dma_start(m0[:], io.state_m.rearrange("b h -> h b")).then_inc(small_in, 16)
            sp.dma_start(io.conv_sample[:, 0:PAD - 1, :], io.state_conv[:, 1:PAD, :]).then_inc(carried, 16)

            def keep(h):
                sp.wait_ge(xm_ready, 2 * FH * (h + 1))
                sp.dma_start(io.xm_keep[ds(h, 1)].rearrange("a p f t -> (a p) f t"), xm[:, :, PAD:]).then_inc(xm_kept, 16)
                sp.wait_ge(xc_ready, 2 * FH * (h + 1))
                sp.dma_start(io.xc_keep[ds(h, 1)].rearrange("a p f t -> (a p) f t"), xc[:]).then_inc(xc_kept, 16)

            def store_rows(h):
                sp.wait_ge(rows_taken, h + 1)
                sp.dma_start(io.conv_prompt[:, ds(h * M_DIM, M_DIM)], last_rows[0:PAD, :]).then_inc(rows_stored, 16)
                sp.dma_start(io.conv_sample[:, PAD - 1, ds(h * M_DIM, M_DIM)], last_rows[PAD:, :]).then_inc(rows_stored, 16)

            with sp.Fori(0, M_HEADS - 1) as i:
                load_w(i + 1)
                keep(i)
                store_rows(i)
            keep(M_HEADS - 1)
            store_rows(M_HEADS - 1)
            sp.wait_ge(gate_ready, 1)
            sp.dma_start(fg[:], gate[M_HEADS:2 * M_HEADS, :]).then_inc(f_moved, 16)
            sp.wait_ge(m_ready, 1)
            sp.dma_start(io.gate_rows[0], bm[:, 0:SEQ]).then_inc(row_out, 16)
            sp.dma_start(io.gate_rows[1], ib[:, 0:SEQ]).then_inc(row_out, 16)
            sp.dma_start(io.gate_rows[2], m_run[:, 0:SEQ]).then_inc(row_out, 16)
            sp.dma_start(io.m_prompt, m_run[:, SEQ - 1:SEQ]).then_inc(row_out, 16)
            sp.dma_start(io.m_sample.rearrange("b h -> h b"), m_run[:, SEQ:TOK]).then_inc(row_out, 16)
            sp.wait_ge(steps_ready, 1)
            sp.dma_start(io.step_rows.rearrange("s h b -> h s b"), steps[:]).then_inc(row_out, 16)
            sp.wait_ge(row_out, 16 * 6)
            sp.wait_ge(carried, 16)
            sp.wait_ge(rows_stored, 32 * M_HEADS)
            sp.wait_ge(xm_kept, 16 * M_HEADS)
            sp.wait_ge(xc_kept, 16 * M_HEADS)

        @block.scalar
        def _(act):
            wide = io.m_w_if.rearrange("(s f g o) n -> s g f (o n)", s=3, f=MF, o=4)
            for i in range(4):
                for s in range(3):
                    act.dma_start(w_if[i::4, s].rearrange("p f o n -> p f (o n)"), wide[s]).then_inc(w_if_in, 16)
            for s, v in enumerate((io.m_w_q, io.m_w_k, io.m_w_v)):
                act.dma_start(c.w_blk[:, s], v.rearrange("(f p) o -> p f o", p=P)).then_inc(blk_in, 16)

            def take(h, f):
                for s in range(2):
                    if s == 0 and not isinstance(h, int):
                        act.wait_ge(gates_done, FH * (h - 1) + f + 1)
                        act.wait_ge(conv_ready, 2 * (FH * (h - 1) + f + 1))
                        if f == 0:
                            act.wait_ge(xm_kept, 16 * h)
                            act.wait_ge(rows_turned, h)
                    act.wait_ge(proj, 2 * (FH * h + f) + s + 1)
                    nc.scalar.copy(xm[:, f, PAD + s * HALF:PAD + (s + 1) * HALF],
                                   xm_ps[:, 2 * (f % 2) + s, 0:HALF]).then_inc(xm_ready, 1)

            def tanh(h, f):
                act.wait_ge(conv_ready, 2 * (FH * h + f) + 2)
                need(act, xc_ready, 2 * (FH * h + f) - 2)
                nc.scalar.activation(th[:, f % 2, :], u[:, f, :], ACT.Tanh).then_inc(tanh_ready, 1)

            def head(h):
                take(h, 0)
                for f in range(1, FH):
                    take(h, f)
                    tanh(h, f - 1)
                tanh(h, FH - 1)

            def take_rows(h):
                act.wait_ge(rows_turned, h + 1)
                need(act, rows_stored, 32 * h)
                nc.scalar.copy(last_rows[:], row_ps[0:PAD + DEC, :]).then_inc(rows_taken, 1)

            act.wait_ge(vec_turned, 1)
            nc.scalar.mul(c.vec[:, 0:(CONV + 1) * MF], prep_ps[:, 0:(CONV + 1) * MF], 0.5).then_inc(vec_ready, 1)
            nc.scalar.copy(c.vec[:, (CONV + 1) * MF:], prep_ps[:, (CONV + 1) * MF:N_VEC]).then_inc(vec_ready, 1)
            act.wait_ge(st_turned, 1)
            nc.scalar.copy(st[:].rearrange("p f b j -> p (f b j)"), row_ps[:, 0:MF * DEC * PAD]).then_inc(st_ready, 1)
            head(0)
            take_rows(0)
            with act.Fori(1, M_HEADS) as h:
                head(h)
                take_rows(h)
            act.wait_ge(gate_ready, 2)
            nc.scalar.activation(na[:], na[:], ACT.Exp).then_inc(exp_ready, 1)
            act.wait_ge(exp_ready, 1)
            nc.scalar.activation(na[:], na[:], ACT.Ln, bias=1.0).then_inc(exp_ready, 1)
            act.wait_ge(gate_ready, 3)
            nc.scalar.activation(steps[:], steps[:], ACT.Exp).then_inc(steps_ready, 1)

        @block.gpsimd
        def _(pool):
            nc.gpsimd.memset(xm[:, :, 0:PAD], 0.0).then_inc(zeroed, 1)
            nc.gpsimd.memset(zero[:], 0.0).then_inc(zeroed, 1)
            nc.gpsimd.memset(ones[:], 1.0).then_inc(zeroed, 1)
            nc.gpsimd.memset(u[:, 0, :], 0.0).then_inc(zeroed, 1)
            nc.gpsimd.memset(c.in_block[:], 1.0).then_inc(zeroed, 1)
            pool.wait_ge(zeroed, 5)
            nc.gpsimd.affine_select(out=c.in_block[:], in_=c.in_block[:], compare_op=ALU.is_ge, fill=0.0, base=0,
                                    pattern=[[-4, P // 4], [0, 4]], channel_multiplier=1).then_inc(zeroed, 1)
            pool.wait_ge(zeroed, 6)
            nc.gpsimd.affine_select(out=c.in_block[:], in_=c.in_block[:], compare_op=ALU.is_ge, fill=0.0, base=3,
                                    pattern=[[4, P // 4], [0, 4]], channel_multiplier=-1).then_inc(zeroed, 1)
            pool.wait_ge(zeroed, 7)

        @block.vector
        def _(dve):
            chain = Chain(dve, step)
            dve.wait_ge(w_if_in, 16 * 12)
            dve.wait_ge(blk_in, 16 * 3)
            for s in range(3):
                last = nc.vector.tensor_tensor(w_fold[:, s], w_if[:, s],
                                               c.w_blk[:, s].unsqueeze(3).broadcast_to([P, MF, 4, 2 * M_HEADS]), ALU.mult)
            chain(last)
            for s in range(3):
                last = nc.vector.tensor_reduce(w_eff2[:, s], w_fold[:, s].rearrange("p f o n -> p f n o"), AX_X, ALU.add)
            chain(last)
            nc.vector.tensor_tensor(w_eff[:, 0], w_eff2[:, 0], w_eff2[:, 1], ALU.add)
            chain(nc.vector.tensor_copy(w_eff[:, 1], w_eff2[:, 2]))
            dve.wait_ge(vec_ready, 2)
            dve.wait_ge(st_ready, 1)
            dve.wait_ge(zeroed, 7)

            def tap(j, h, f):
                return c.vec[:, ds(j * MF + h * FH + f, 1)]

            def head(h):
                for f in range(FH):
                    dve.wait_ge(xm_ready, 2 * (FH * h + f) + 2)
                    past = st[:, ds(h * FH + f, 1), :, :].rearrange("p a b j -> p (a b) j")
                    a, s = u[:, f, 0:SEQ], u[:, f, SEQ:TOK]
                    nc.vector.tensor_scalar(a, xm[:, f, 0:SEQ], tap(0, h, f), tap(CONV, h, f), ALU.mult, ALU.add)
                    chain(nc.vector.tensor_scalar(s, past[:, :, 0], tap(0, h, f), tap(CONV, h, f), ALU.mult, ALU.add))
                    for j in range(1, CONV):
                        src = xm[:, f, S0:S0 + DEC] if j == PAD else past[:, :, j]
                        i1 = nc.vector.scalar_tensor_tensor(out=a, in0=xm[:, f, j:j + SEQ], scalar=tap(j, h, f), in1=a,
                                                            op0=ALU.mult, op1=ALU.add)
                        i2 = nc.vector.scalar_tensor_tensor(out=s, in0=src, scalar=tap(j, h, f), in1=s,
                                                            op0=ALU.mult, op1=ALU.add)
                        if j < PAD:
                            chain(i2)
                    i1.then_inc(conv_ready, 1)
                    i2.then_inc(conv_ready, 1)
                    if f:
                        silu(h, f - 1)
                silu(h, FH - 1)

            def silu(h, f):
                dve.wait_ge(tanh_ready, FH * h + f + 1)
                if not isinstance(h, int):
                    dve.wait_ge(gates_done, FH * (h - 1) + f + 1)
                    dve.wait_ge(xc_kept, 16 * h)
                nc.vector.scalar_tensor_tensor(out=xc[:, f, :], in0=th[:, f % 2, :], scalar=1.0, in1=u[:, f, :],
                                               op0=ALU.add, op1=ALU.mult).then_inc(xc_ready, 2)

            def share(h):
                if not isinstance(h, int):
                    need_apart(dve, gates_done, FH * h, tick)
                nc.vector.tensor_copy(w_now[:], w_eff[:, :, ds(h * FH, FH), :]).then_inc(now_ready, 1)

            share(0)
            head(0)
            with dve.Fori(1, M_HEADS) as h:
                chain.enter(h - 1, FH * 3)
                head(h)
                share(h)
                chain.leave(M_HEADS - 1)

            dve.wait_ge(small_in, 32)
            dve.wait_ge(gates_done, FH * M_HEADS)
            halves = [gate[:, s * HALF:(s + 1) * HALF] for s in range(2)]
            for s in range(2):
                last = nc.vector.tensor_scalar(halves[s], gate_ps[QUADS[s], 0:HALF], bias[:, 0:1], None, ALU.add)
            chain(last)
            for s in range(2):
                last = nc.vector.tensor_tensor(halves[s], halves[s], gate_ps[QUADS[2 + s], 0:HALF], ALU.add)
            last.then_inc(gate_ready, 1)
            dve.wait_ge(f_moved, 16)
            chain(nc.vector.tensor_scalar(na[:], fg[:], -1.0, None, ALU.mult))
            nc.vector.tensor_tensor(na[:], na[:], fg[:], ALU.min).then_inc(gate_ready, 1)
            dve.wait_ge(exp_ready, 2)
            chain(nc.vector.scalar_tensor_tensor(out=lf[:], in0=fg[:], scalar=0.0, in1=na[:], op0=ALU.min,
                                                 op1=ALU.subtract))
            ig = gate[0:M_HEADS, :]
            nc.vector.tensor_tensor_scan(b_sum[:, 0:SEQ], ones[:, 0:SEQ], lf[:, 0:SEQ], 0.0, ALU.mult, ALU.add)
            nc.vector.tensor_tensor_scan(m_run[:, 0:SEQ], lf[:, 0:SEQ], ig[:, 0:SEQ], 0.0, ALU.add, ALU.max)
            chain(nc.vector.tensor_tensor(inter[:], lf[:, SEQ:TOK], m0[:], ALU.add))
            chain(nc.vector.tensor_tensor(m_run[:, SEQ:TOK], inter[:], ig[:, SEQ:TOK], ALU.max))
            nc.vector.tensor_tensor(bm[:, 0:SEQ], b_sum[:, 0:SEQ], m_run[:, 0:SEQ], ALU.subtract)
            nc.vector.tensor_tensor(ib[:, 0:SEQ], ig[:, 0:SEQ], b_sum[:, 0:SEQ], ALU.subtract).then_inc(m_ready, 1)
            nc.vector.tensor_tensor(steps[:, 0, :], inter[:], m_run[:, SEQ:TOK], ALU.subtract)
            nc.vector.tensor_tensor(steps[:, 1, :], ig[:, SEQ:TOK], m_run[:, SEQ:TOK], ALU.subtract)
            nc.vector.tensor_scalar(steps[:, 2, :], m_run[:, SEQ:TOK], -1.0, None, ALU.mult).then_inc(gate_ready, 1)

        @block.tensor
        def _(pe):
            pe.wait_ge(vec_in, 16 * 4)
            nc.tensor.transpose(prep_ps[:, 0:N_VEC], vec[:], c.ident[0:N_VEC, 0:N_VEC]).then_inc(vec_turned, 1)
            pe.wait_ge(st_in, 16)
            n_st = DEC * PAD
            for f in range(MF):
                last = nc.tensor.transpose(row_ps[:, f * n_st:(f + 1) * n_st], st_rows[:, f * P:(f + 1) * P],
                                           c.ident[0:n_st, 0:n_st])
            last.then_inc(st_turned, 1)
            pe.wait_ge(st_ready, 1)
            pe.wait_ge(zeroed, 7)
            for j in range(4):
                nc.tensor.matmul(gate_ps[QUADS[j], 0:HALF], zero[:], u[:, 0, 0:HALF], start=True, stop=True)

            def project(h, f):
                if f % 2 == 0:
                    pe.wait_ge(w_in[f // 2], 16 * (h + 1))
                if isinstance(h, int):
                    need(pe, xm_ready, 2 * (FH * h + f) - 2)
                else:
                    pe.wait_ge(xm_ready, 2 * (FH * h + f) - 2)
                for s in range(2):
                    for k in range(KT):
                        last = nc.tensor.matmul(xm_ps[:, 2 * (f % 2) + s, 0:HALF],
                                                w[:, f // 2, k, (f % 2) * P:(f % 2 + 1) * P],
                                                c.hT[:, k, s * HALF:(s + 1) * HALF], start=(k == 0), stop=(k == KT - 1))
                    last.then_inc(proj, 1)
                if f % 2:
                    pe.wait_ge(proj, 2 * (FH * h + f) + 2)
                    pe.sem_inc(w_used, 1)

            def gates(h, f):
                if f == 0:
                    pe.wait_ge(xm_ready, 2 * FH * (h + 1))
                    need(pe, rows_taken, h)
                    for g in range(FH):
                        last = nc.tensor.transpose(row_ps[0:PAD + DEC, g * P:(g + 1) * P], xm[:, g, SEQ:SEQ + PAD + DEC],
                                                   c.ident[:])
                    last.then_inc(rows_turned, 1)
                    pe.wait_ge(now_ready, h + 1)
                pe.wait_ge(xc_ready, 2 * (FH * h + f) + 2)
                for n, src in enumerate((xc[:, f, :], xm[:, f, PAD:])):
                    for s in range(2):
                        last = nc.tensor.matmul(gate_ps[QUADS[2 * n + s], 0:HALF], w_now[:, n, f, :],
                                                src[:, s * HALF:(s + 1) * HALF], start=False, stop=True,
                                                skip_group_check=True)
                last.then_inc(gates_done, 1)

            for f in range(FH):
                project(0, f)
            for f in range(FH):
                gates(0, f)
                project(1, f)
            with pe.Fori(1, M_HEADS - 1) as h:
                for f in range(FH):
                    gates(h, f)
                    project(h + 1, f)
            for f in range(FH):
                gates(M_HEADS - 1, f)


def build_mlstm(nc, c, io):
    Z, Q, K = 0, 2 * FH, 4 * FH
    COLS = 6 * FH
    TOK_TURNS = (["act"] * 2
                 + ["act"] * TT
                 + ["dve"] * NT
                 + ["dve"] * NT
                 + ["act"] * NT
                 + ["dve"]
                 + ["dve"] * NT
                 + ["act"] * FH
                 + ["dve"]
                 + ["dve"] * TT)
    ROWS, V, KD, SC, OG, NUM, CP, SNUM, HT = 0, 2, 7, 11, 15, 20, 24, 28, 29
    TOKS = len(TOK_TURNS)
    PER = {e: TOK_TURNS.count(e) for e in ("act", "dve")}
    PIECES = 2 * DEC
    with ExitStack() as ctx:
        m = Mem(nc, ctx)
        wz = m.sb("w_z", [P, 2, KT, P])
        wg = m.sb("w_og", [P, KT, M_DIM])
        xc = m.sb("xc_head", [P, FH, TOK])
        xm = m.sb("xm_head", [P, FH, TOK])
        st = xm
        blk = m.sb("blk", [P, 3, FH, P])
        qT = m.sb("qT_m", [P, FH, TOK])
        kT = m.sb("kT_m", [P, FH, TOK])
        v = m.sb("v_m", [P, TT, M_DIM])
        kd = m.sb("kd", [P, NT, M_DIM])
        og = m.sb("og", [P, TT, M_DIM])
        th = m.sb("th_z", [P, 2, HALF])
        fac = m.sb("fac", [P, 2, SEQ])
        bm = m.sb("bm_bcast", [P, SEQ])
        bm_diag = m.sb("bm_diag", [P, NT, P])
        ib = m.sb("ib_col", [P, M_HEADS, NT])
        em = m.sb("em_col", [P, M_HEADS, NT])
        dec = m.sb("dec_col", [P, M_HEADS, NT])
        bm_end = m.sb("bm_end", [P, M_HEADS])
        s_all = m.sb("s_all", [P, 3, M_HEADS, DEC])
        s_row = m.sb("s_row", [DEC, 3, M_HEADS])
        state = m.sb("state", [P, 4, 2, M_DIM])
        outer = m.sb("outer", [P, 2, 2, M_DIM])
        vb = m.sb("v_bcast", [P, 2, M_DIM])
        kc = m.sb("k_cols", [P, FH, DEC])
        qm = m.sb("q_mask", [P, FH, DEC * 32])
        sn = m.sb("sn", [P, M_DIM])
        sum4 = m.sb("sum4", [P, DEC])
        one = m.sb("one_col", [P, 1])
        krow, qrow, nrow = (m.sb(n, [DEC, M_DIM]) for n in ("krow", "qrow", "nrow"))
        junk = m.sb("junk", [DEC, M_DIM])
        c_out = m.sb("c_out", [P, 2, M_DIM])
        n_out = m.sb("n_out", [P, FH])
        qn = m.sb("qn_s", [DEC, 1])
        rd, var, mu_r = (m.sb(n, [P, TT]) for n in ("rd", "var", "rstd_ln"))
        stats = m.sb("stats", [P, 6])
        mv = m.sb("mv", [P, TT, 2])
        gain = m.sb("gain_now", [P, 2, FH])
        mix = m.sb("mix", [P, 2, FH, P])
        upper = m.sb("upper", [P, P])
        col_ps = m.ps("col_ps", [P, 4, 512])
        tok_ps = m.ps("tok_ps", [P, 2, 512])
        sn_ps = m.ps("sn_ps", [P, 512])
        q_ps = m.ps("q_ps", [P, 512])
        z_in = [m.sem(f"z_in{j}_d") for j in range(2)]
        st_in = [m.sem(f"state_in{j}_d") for j in range(4)]
        st_out = [m.sem(f"state_out{j}_d") for j in range(4)]
        vb_in = [m.sem(f"v_bcast_in{j}_d") for j in range(2)]
        cp_out = [m.sem(f"cp_out{j}_d") for j in range(2)]
        (z_used, og_summed, og_tanh, og_in, xc_in, xm_in, bm_in, n_in, pre_in, cols_done, cols_act, cols_dve, z_tanh, toks_done, toks_act,
         toks_dve, fac_ready, diag_ready, blk_ready, qk_used, skip_ready, consts, cols_exp, kq_ready, v_kept,
         outer_ready, new_ready, sn_used, sn_taken, n_done, n_taken, n_stored, nrow_ready, nrow_used, ns_stored, ln_var,
         ln_rstd, ln_done, chained, pool_tick, dve_tick, pe_tick) = (m.sem(n + "_d") for n in (
             "z_used", "og_summed", "og_tanh", "og_in", "xc_in", "xm_in", "bm_in", "n_in", "pre_in", "cols_done", "cols_act", "cols_dve",
             "z_tanh", "toks_done", "toks_act", "toks_dve", "fac_ready", "diag_ready", "blk_ready", "qk_used",
             "skip_ready", "consts", "cols_exp", "kq_ready", "v_kept", "outer_ready", "new_ready", "sn_used",
             "sn_taken", "n_done", "n_taken", "n_stored", "nrow_ready", "nrow_used", "ns_stored", "ln_var", "ln_rstd",
             "ln_done", "chained", "pool_tick", "dve_tick", "pe_tick"))
        taken = {"act": toks_act, "dve": toks_dve}
        w_view = io.m_w_in.rearrange("(k p) n -> p k n", p=P)
        block = m.block()

        def tok_count(h, u):
            e = TOK_TURNS[u]
            return taken[e], PER[e] * h + TOK_TURNS[:u + 1].count(e)

        def col_count(h, u):
            return (cols_dve, 2 * FH * h + u + 1) if u < Q else (cols_act, 4 * FH * h + u - Q + 1)

        @block.sync
        def _(sp):
            sp.dma_start(ib[:].rearrange("p h t -> p (h t)"), io.gate_rows[1].rearrange("h (t p) -> p (h t)", p=P)).then_inc(pre_in, 16)
            sp.dma_start(em[:].rearrange("p h t -> p (h t)"), io.gate_rows[2].rearrange("h (t p) -> p (h t)", p=P)).then_inc(pre_in, 16)
            sp.dma_start(bm_end[:], io.gate_rows[0, :, SEQ - 1].partition_broadcast(P)).then_inc(pre_in, 16)
            sp.dma_start(s_all[:].rearrange("p s h b -> p (s h b)"),
                         io.step_rows.rearrange("s h b -> (s h b)").partition_broadcast(P)).then_inc(pre_in, 16)
            sp.dma_start(s_row[:], io.step_rows.rearrange("s h b -> b s h")).then_inc(pre_in, 16)

            def half(arr, h, k):
                b, g = divmod(k, 2)
                return arr[b, ds(h, 1)].rearrange("a (g d p) e -> p g (a d) e", g=2, p=P)[:, g]

            def load_state(h, k):
                sp.dma_start(state[:, k % 4], half(io.state_C, h, k)).then_inc(st_in[k % 4], 16)

            def load_vb(h, b):
                sp.dma_start(vb[:, b % 2, :], io.v_rows[ds(h, 1), b * M_DIM:(b + 1) * M_DIM].rearrange("a n -> (a n)")
                             .partition_broadcast(P)).then_inc(vb_in[b % 2], 16)

            def head(h, last=False):
                sem, n = tok_count(h, V + NT)
                sp.wait_ge(sem, n)
                sp.dma_start(io.v_rows[ds(h, 1)].rearrange("a (b n) -> (a b) n", b=DEC), v[0:DEC, NT, :]).then_inc(v_kept, 16)
                sp.wait_ge(v_kept, 16 * (h + 1))
                load_vb(h, 0)
                load_vb(h, 1)
                for k in range(PIECES):
                    sp.wait_ge(new_ready, PIECES * h + k + 1)
                    sp.dma_start(half(io.C_sample, h, k), state[:, k % 4]).then_inc(st_out[k % 4], 16)
                    if k % 2 and k // 2 + 2 < DEC:
                        load_vb(h, k // 2 + 2)
                    if not (last and k + 3 >= PIECES):
                        if k > 0 or not isinstance(h, int) or h > 0:
                            sp.wait_ge(st_out[(k - 1) % 4], 16 * (4 * h + (k - 1) // 4 + 1))
                            sp.wait_ge(sn_used, PIECES * h + k)
                        load_state(h if k + 3 < PIECES else h + 1, (k + 3) % PIECES)

            for k in range(3):
                load_state(0, k)
            head(0)
            with sp.Fori(1, M_HEADS - 1) as h:
                head(h)
            head(M_HEADS - 1, last=True)
            for s in st_out:
                sp.wait_ge(s, 16 * PIECES * M_HEADS // 4)

        @block.gpsimd
        def _(pool):
            nc.gpsimd.memset(upper[:], 0.0).then_inc(consts, 1)
            nc.gpsimd.memset(qm[:], 0.0).then_inc(consts, 1)
            nc.gpsimd.memset(sum4[:], 0.0).then_inc(consts, 1)
            nc.gpsimd.memset(one[:], 1.0).then_inc(consts, 1)
            pool.wait_ge(consts, 4)
            nc.gpsimd.affine_select(out=upper[:], in_=upper[:], compare_op=ALU.is_ge, fill=MASKED, base=0,
                                    pattern=[[1, P]], channel_multiplier=-1).then_inc(consts, 1)
            for j in range(4):
                nc.gpsimd.affine_select(out=sum4[:], in_=sum4[:], compare_op=ALU.not_equal, fill=1.0, base=-32 * j,
                                        pattern=[[-1, DEC]], channel_multiplier=1).then_inc(consts, 1)
                pool.wait_ge(consts, 6 + j)

            def load_z(h, f):
                if f < 2:
                    if not isinstance(h, int) or h > 0:
                        need_apart(pool, z_used, FH * h + f - 1, pool_tick)
                else:
                    need_apart(pool, z_used, FH * h + f - 1, pool_tick)
                pool.dma_start(wz[:, f % 2], w_view[:, :, ds(2 * M_WIDTH + h * M_DIM + f * P, P)]).then_inc(z_in[f % 2], 16)

            def load_og(h):
                pool.dma_start(wg[:], w_view[:, :, ds(M_WIDTH + h * M_DIM, M_DIM)]).then_inc(og_in, 16)

            def load_rows(h):
                pool.dma_start(bm[:], io.gate_rows[0, ds(h, 1), :].rearrange("a n -> (a n)").partition_broadcast(P)).then_inc(bm_in, 16)
                pool.dma_start(nrow[:], io.state_n[:, ds(h * M_DIM, M_DIM)]).then_inc(n_in, 16)

            def load_xm(h):
                pool.dma_start(xm[:], io.xm_keep[ds(h, 1)].rearrange("a p f t -> (a p) f t")).then_inc(xm_in, 16)

            def load_xc(h):
                pool.dma_start(xc[:], io.xc_keep[ds(h, 1)].rearrange("a p f t -> (a p) f t")).then_inc(xc_in, 16)

            def head(h, last=False):
                load_z(h, 2)
                load_z(h, 3)
                pool.wait_ge(toks_done, TOKS * h + V + TT)
                nc.gpsimd.tensor_tensor(xc[:], xc[:], gain[:, 1, :].unsqueeze(2).broadcast_to([P, FH, TOK]),
                                        ALU.mult).then_inc(skip_ready, 1)
                need_apart(pool, nrow_ready, h + 1, pool_tick)
                pool.dma_start(io.n_sample[:, ds(h * M_DIM, M_DIM)], nrow[:]).then_inc(ns_stored, 16)
                if not last:
                    load_z(h + 1, 0)
                    load_z(h + 1, 1)
                    need_apart(pool, toks_done, TOKS * h + OG + TT, pool_tick)
                    load_og(h + 1)
                for t in range(TT):
                    pool.wait_ge(ln_var, TT * h + t + 1)
                    nc.gpsimd.tensor_tensor(mu_r[0:rows(t), t:t + 1], var[0:rows(t), t:t + 1],
                                            c.minus_half[0:rows(t), 0:1], ALU.pow).then_inc(ln_rstd, 1)
                if not last:
                    need_apart(pool, toks_done, TOKS * h + NUM + NT, pool_tick)
                    load_xm(h + 1)
                    need_apart(pool, fac_ready, NT * h + NT, pool_tick)
                    need_apart(pool, nrow_used, h + 1, pool_tick)
                    need_apart(pool, ns_stored, 16 * (h + 1), pool_tick)
                    load_rows(h + 1)
                    need_apart(pool, toks_dve, PER["dve"] * (h + 1), pool_tick)
                    load_xc(h + 1)

            load_z(0, 0)
            load_z(0, 1)
            load_xc(0)
            load_xm(0)
            load_rows(0)
            load_og(0)
            head(0)
            with pool.Fori(1, M_HEADS - 1) as h:
                head(h)
            head(M_HEADS - 1, last=True)
            pool.wait_ge(ns_stored, 16 * M_HEADS)

        @block.scalar
        def _(act):
            act.wait_ge(pre_in, 16 * 5)
            nc.scalar.activation(em[:], em[:], ACT.Exp, scale=-1.0).then_inc(cols_exp, 1)
            for h in range(M_HEADS):
                last = nc.scalar.activation(dec[:, h, :], ib[:, h, :], ACT.Exp, bias=bm_end[:, h:h + 1])
            last.then_inc(cols_exp, 1)

            def z(h, u):
                act.wait_ge(cols_done, COLS * h + u + 1)
                need(act, cols_dve, 2 * FH * h + u - 1)
                nc.scalar.activation(th[:, u % 2, :], col_ps[:, u % 4, 0:HALF], ACT.Tanh, scale=0.5).then_inc(z_tanh, 1)

            def qk(h, u):
                f, s = divmod((u - Q) % (2 * FH), 2)
                act.wait_ge(cols_done, COLS * h + u + 1)
                src = col_ps[:, u % 4, 0:HALF]
                if u < K:
                    nc.scalar.copy(qT[:, f, s * HALF:(s + 1) * HALF], src).then_inc(cols_act, 1)
                else:
                    nc.scalar.mul(kT[:, f, s * HALF:(s + 1) * HALF], src, K_SCALE).then_inc(cols_act, 1)

            def take(h, u, dst, p, mul=None):
                act.wait_ge(toks_done, TOKS * h + u + 1)
                src = tok_ps[0:p, u % 2, :]
                if mul is None:
                    nc.scalar.copy(dst, src).then_inc(toks_act, 1)
                else:
                    nc.scalar.mul(dst, src, mul).then_inc(toks_act, 1)

            def factors(h, s):
                if s == 0:
                    act.wait_ge(diag_ready, h + 1)
                bias = c.ib_now[:, s:s + 1]
                need(act, toks_dve, PER["dve"] * h + NT + s - 1)
                last = nc.scalar.activation(fac[:, s % 2, s * P:(s + 1) * P], bm_diag[:, s, :], ACT.Exp, bias=bias)
                if s < NT - 1:
                    last = nc.scalar.activation(fac[:, s % 2, (s + 1) * P:], bm[:, (s + 1) * P:], ACT.Exp, bias=bias)
                last.then_inc(fac_ready, 1)

            def outer_of(h, b):
                if b == 0:
                    act.wait_ge(kq_ready, h + 1)
                act.wait_ge(vb_in[b % 2], 16 * (4 * h + b // 2 + 1))
                for g in range(2):
                    need(act, new_ready, PIECES * h + 2 * b + g - 1)
                    for d in range(2):
                        last = nc.scalar.activation(outer[:, g, d, :], vb[:, b % 2, :], ACT.Copy,
                                                    scale=kc[:, 2 * g + d, b:b + 1])
                    last.then_inc(outer_ready, 1)

            def out_gate(h, t):
                if t == NT:
                    g = og[0:DEC, NT, :]
                    act.wait_ge(og_summed, h + 1)
                    nc.scalar.activation(g, g, ACT.Tanh, scale=0.5).then_inc(og_tanh, 1)
                    return
                act.wait_ge(toks_done, TOKS * h + OG + t + 1)
                if t == 0:
                    need(act, toks_done, TOKS * h)
                nc.scalar.activation(og[0:rows(t), t, :], tok_ps[0:rows(t), (OG + t) % 2, :], ACT.Tanh,
                                     scale=0.5).then_inc(toks_act, 1)

            def prompt_state(h, d):
                if not (isinstance(h, int) and h == 0 and d < 2):
                    act.wait_ge(cp_out[d % 2], 16 * (2 * h + d // 2))
                take(h, CP + d, c_out[:, d % 2, :], P)
                act.wait_ge(toks_act, PER["act"] * h + PER["act"] - FH + d + 1)
                act.dma_start(io.C_prompt[ds(h, 1), d * P:(d + 1) * P, :].rearrange("a p e -> (a p) e"),
                              c_out[:, d % 2, :]).then_inc(cp_out[d % 2], 16)

            def head(h):
                for u in range(2 * FH):
                    z(h, u)
                for u in range(Q, COLS):
                    qk(h, u)
                need(act, nrow_used, h)
                take(h, ROWS, qrow[:], DEC)
                take(h, ROWS + 1, krow[:], DEC, K_SCALE)
                for t in range(TT):
                    take(h, V + t, v[0:rows(t), t, :], rows(t))
                for s in range(NT):
                    factors(h, s)
                for t in range(TT):
                    outer_of(h, t)
                    out_gate(h, t)
                outer_of(h, 5)
                outer_of(h, 6)
                prompt_state(h, 0)
                outer_of(h, 7)
                for d in range(1, FH):
                    prompt_state(h, d)
                act.wait_ge(n_done, h + 1)
                need(act, n_stored, 16 * h)
                nc.scalar.copy(n_out[:], q_ps[:, FH:2 * FH]).then_inc(n_taken, 1)
                act.wait_ge(n_taken, h + 1)
                act.dma_start(io.n_prompt[ds(h, 1)].rearrange("a (d p) -> p (a d)", p=P), n_out[:]).then_inc(n_stored, 16)

            head(0)
            with act.Fori(1, M_HEADS) as h:
                head(h)
            act.wait_ge(n_stored, 16 * M_HEADS)
            for s in cp_out:
                act.wait_ge(s, 16 * 2 * M_HEADS)

        @block.vector
        def _(dve):
            chain = Chain(dve, chained)

            def prepare(h):
                need_apart(dve, toks_done, TOKS * h, dve_tick)
                need_apart(dve, cols_exp, 2, dve_tick)
                nc.vector.tensor_copy(gain[:], c.vec[:, (CONV + 1) * MF:].rearrange("p (n f) -> p n f", n=2)[:, :, ds(h * FH, FH)])
                nc.vector.tensor_copy(c.ib_now[:], ib[:, ds(h, 1), :].rearrange("p a t -> p (a t)"))
                for s in range(3):
                    w4 = c.w_blk[:, s, ds(h * FH, FH), :].unsqueeze(2).broadcast_to([P, FH, P // 4, 4])
                    last = nc.vector.tensor_tensor(blk[:, s].rearrange("p f (g o) -> p f g o", o=4), w4,
                                                   c.in_block[:].unsqueeze(1).broadcast_to([P, FH, P // 4, 4]), ALU.mult)
                last.then_inc(blk_ready, 1)
                dve.wait_ge(bm_in, 16 * (h + 1))
                nc.vector.tensor_tensor(bm_diag[:], bm[:].rearrange("p (t q) -> p t q", t=NT),
                                        upper[:].unsqueeze(1).broadcast_to([P, NT, P]), ALU.add).then_inc(diag_ready, 1)

            def z(h, u):
                f, s = divmod(u, 2)
                dve.wait_ge(z_tanh, 2 * FH * h + u + 1)
                nc.vector.scalar_tensor_tensor(out=c.gated[:, ds(h * FH + f, 1), s * HALF:(s + 1) * HALF].rearrange("p a t -> p (a t)"),
                                               in0=th[:, u % 2, :], scalar=1.0, in1=col_ps[:, u % 4, 0:HALF],
                                               op0=ALU.add, op1=ALU.mult).then_inc(cols_dve, 1)

            def sample_columns(h):
                dve.wait_ge(cols_act, 4 * FH * (h + 1))
                nc.vector.tensor_tensor(kc[:], kT[:, :, SEQ:TOK],
                                        s_all[:, 1, ds(h, 1), :].broadcast_to([P, FH, DEC]), ALU.mult)
                nc.vector.tensor_copy(qm[:, :, 0:33 * (DEC - 1) + 1:33], qT[:, :, SEQ:TOK]).then_inc(kq_ready, 1)

            def sample_n(h):
                dve.wait_ge(n_in, 16 * (h + 1))
                sem, n = tok_count(h, ROWS + 1)
                dve.wait_ge(sem, n)
                chain(nc.vector.tensor_scalar(nrow[:], nrow[:], s_row[:, 0, ds(h, 1)], None, ALU.mult))
                nc.vector.scalar_tensor_tensor(out=nrow[:], in0=krow[:], scalar=s_row[:, 1, ds(h, 1)], in1=nrow[:],
                                               op0=ALU.mult, op1=ALU.add).then_inc(nrow_ready, 1)
                dve.wait_ge(nrow_ready, h + 1)
                chain(nc.vector.tensor_tensor_reduce(out=junk[:], in0=qrow[:], in1=nrow[:], scale=1.0, scalar=0.0,
                                                     op0=ALU.mult, op1=ALU.add, accum_out=qn[:, 0:1]))
                chain(nc.vector.tensor_scalar(rd[0:DEC, NT:TT], qn[:, 0:1], -1.0, s_row[:, 2, ds(h, 1)], ALU.mult, ALU.max))
                chain(nc.vector.tensor_scalar(rd[0:DEC, NT:TT], qn[:, 0:1], rd[0:DEC, NT:TT], 2.0, ALU.max, ALU.mult))
                nc.vector.reciprocal(rd[0:DEC, NT:TT], rd[0:DEC, NT:TT]).then_inc(nrow_used, 1)

            def decayed(h, t):
                dve.wait_ge(toks_done, TOKS * h + KD + t + 1)
                nc.vector.tensor_scalar(kd[:, t, :], tok_ps[:, (KD + t) % 2, :], dec[:, ds(h, 1), t], None,
                                        ALU.mult).then_inc(toks_dve, 1)

            def weigh(h, s):
                dve.wait_ge(toks_done, TOKS * h + SC + s + 1)
                dve.wait_ge(fac_ready, NT * h + s + 1)
                nc.vector.tensor_tensor(st[:, s, s * P:SEQ], tok_ps[:, (SC + s) % 2, s * P:], fac[:, s % 2, s * P:],
                                        ALU.mult).then_inc(toks_dve, 1)

            def sum_og(h):
                u = OG + NT
                dve.wait_ge(toks_done, TOKS * h + u + 1)
                g, bank = og[0:DEC, NT, :], tok_ps[:, u % 2, :]
                chain(nc.vector.tensor_copy(g, bank[QUADS[0], :]))
                for j in (1, 2):
                    chain(nc.vector.tensor_tensor(g, g, bank[QUADS[j], :], ALU.add))
                nc.vector.tensor_tensor(g, g, bank[QUADS[3], :], ALU.add).then_inc(toks_dve, 1)
                sem, n = tok_count(h, u)
                dve.wait_ge(sem, n)
                dve.sem_inc(og_summed, 1)

            def new_state(h, b):
                for g in range(2):
                    k = 2 * b + g
                    dve.wait_ge(outer_ready, PIECES * h + k + 1)
                    dve.wait_ge(st_in[k % 4], 16 * (4 * h + k // 4 + 1))
                    nc.vector.scalar_tensor_tensor(out=state[:, k % 4], in0=state[:, k % 4],
                                                   scalar=s_all[:, 0, ds(h, 1), b], in1=outer[:, g],
                                                   op0=ALU.mult, op1=ALU.add).then_inc(new_ready, 1)

            def norm_h(h, t):
                p = rows(t)
                u = NUM + t if t < NT else SNUM
                dve.wait_ge(toks_done, TOKS * h + u + 1)
                g = og[0:p, t, :]
                if t == 0:
                    r, q = rd[:, 0:NT], q_ps[:, 0:NT]
                    e = em[:, ds(h, 1), :].rearrange("p a t -> p (a t)")
                    chain(nc.vector.scalar_tensor_tensor(out=r, in0=q, scalar=-1.0, in1=e, op0=ALU.mult, op1=ALU.max))
                    chain(nc.vector.tensor_tensor(r, q, r, ALU.max))
                    chain(nc.vector.reciprocal(r, r))
                    chain(nc.vector.tensor_scalar(r, r, 0.5, None, ALU.mult))
                if t < NT:
                    sem, n = tok_count(h, OG + t)
                    dve.wait_ge(sem, n)
                else:
                    dve.wait_ge(og_tanh, h + 1)
                nc.vector.scalar_tensor_tensor(out=g, in0=g, scalar=1.0, in1=tok_ps[0:p, u % 2, :], op0=ALU.add,
                                               op1=ALU.mult).then_inc(toks_dve, 1)
                dve.wait_ge(toks_dve, PER["dve"] * h + 2 * NT + 1 + t + 1)
                chain(nc.vector.bn_stats(stats[0:p, :], g))
                dve.sem_inc(dve_tick, 1)
                chain(nc.vector.bn_aggr(mv[0:p, t, :], stats[0:p, :]))
                chain(nc.vector.tensor_scalar(var[0:p, t:t + 1], mv[0:p, t, 1:2], rd[0:p, t:t + 1], rd[0:p, t:t + 1],
                                              ALU.mult, ALU.mult))
                nc.vector.tensor_scalar(var[0:p, t:t + 1], var[0:p, t:t + 1], EPS, None, ALU.add).then_inc(ln_var, 1)

            def scale_h(h, t):
                p = rows(t)
                g = og[0:p, t, :]
                dve.wait_ge(ln_rstd, TT * h + t + 1)
                chain(nc.vector.tensor_tensor(rd[0:p, t:t + 1], rd[0:p, t:t + 1], mu_r[0:p, t:t + 1], ALU.mult))
                nc.vector.tensor_scalar(g, g, mv[0:p, t, 0:1], rd[0:p, t:t + 1], ALU.subtract,
                                        ALU.mult).then_inc(ln_done, 1)

            def mix_in(h, t):
                p = rows(t)
                dve.wait_ge(toks_done, TOKS * h + HT + t + 1)
                src = tok_ps[:, (HT + t) % 2, :].rearrange("p (f r) -> p f r", f=FH)[:, :, 0:p]
                chain(nc.vector.tensor_tensor(mix[:, t % 2, :, 0:p], src, gain[:, 0, :].unsqueeze(2).broadcast_to([P, FH, p]),
                                              ALU.mult))
                if t == 0:
                    dve.wait_ge(skip_ready, h + 1)
                chain(nc.vector.tensor_tensor(mix[:, t % 2, :, 0:p], mix[:, t % 2, :, 0:p], xc[:, :, t * P:t * P + p], ALU.add))
                dst = c.gated[:, ds(h * FH, FH), t * P:t * P + p]
                nc.vector.scalar_tensor_tensor(out=dst, in0=mix[:, t % 2, :, 0:p], scalar=0.5, in1=dst, op0=ALU.mult,
                                               op1=ALU.mult).then_inc(toks_dve, 1)

            def head(h):
                prepare(h)
                for u in range(2 * FH):
                    z(h, u)
                sample_columns(h)
                sample_n(h)
                for t in range(NT):
                    decayed(h, t)
                for s in range(NT):
                    weigh(h, s)
                for b in range(5):
                    if b == 4:
                        sum_og(h)
                    new_state(h, b)
                norm_h(h, 0)
                norm_h(h, 1)
                scale_h(h, 0)
                new_state(h, 5)
                norm_h(h, 2)
                scale_h(h, 1)
                norm_h(h, 3)
                new_state(h, 6)
                scale_h(h, 2)
                scale_h(h, 3)
                new_state(h, 7)
                dve.wait_ge(sn_used, PIECES * (h + 1))
                nc.vector.tensor_copy(sn[:], sn_ps[:]).then_inc(sn_taken, 1)
                norm_h(h, NT)
                scale_h(h, NT)
                for t in range(TT):
                    mix_in(h, t)

            dve.wait_ge(consts, 9)
            head(0)
            with dve.Fori(1, M_HEADS) as h:
                chain.enter(h - 1, 41)
                head(h)
                chain.leave(M_HEADS - 1)

        @block.tensor
        def _(pe):
            def free_col(h, u):
                if u >= 4:
                    pe.wait_ge(*col_count(h, u - 4))
                elif not isinstance(h, int):
                    pe.wait_ge(*col_count(h - 1, COLS + u - 4))

            def free_tok(h, u):
                if u >= 2:
                    pe.wait_ge(*tok_count(h, u - 2))
                elif not isinstance(h, int):
                    pe.wait_ge(*tok_count(h - 1, TOKS + u - 2))

            def z(h, f):
                pe.wait_ge(z_in[f % 2], 16 * (2 * h + f // 2 + 1))
                for s in range(2):
                    u = Z + 2 * f + s
                    free_col(h, u)
                    for k in range(KT):
                        last = nc.tensor.matmul(col_ps[:, u % 4, 0:HALF], wz[:, f % 2, k, :],
                                                c.hT[:, k, s * HALF:(s + 1) * HALF], start=(k == 0), stop=(k == KT - 1))
                    last.then_inc(cols_done, 1)
                pe.wait_ge(cols_done, COLS * h + Z + 2 * f + 2)
                pe.sem_inc(z_used, 1)

            def qk(h, n, f):
                for s in range(2):
                    u = (Q, K)[n] + 2 * f + s
                    free_col(h, u)
                    nc.tensor.matmul(col_ps[:, u % 4, 0:HALF], blk[:, n, f, :], xc[:, f, s * HALF:(s + 1) * HALF],
                                     start=True, stop=True).then_inc(cols_done, 1)

            def by_token(h, u, n, t):
                src = xm if n == 2 else xc
                p = rows(t)
                free_tok(h, u)
                for f in range(FH):
                    last = nc.tensor.matmul(tok_ps[0:p, u % 2, f * P:(f + 1) * P], src[:, f, t * P:t * P + p],
                                            blk[:, n, f, :], start=True, stop=True)
                last.then_inc(toks_done, 1)

            def turned_k(h, t):
                u = KD + t
                free_tok(h, u)
                if t == 0:
                    pe.wait_ge(cols_act, 4 * FH * (h + 1))
                for f in range(FH):
                    last = nc.tensor.transpose(tok_ps[:, u % 2, f * P:(f + 1) * P], kT[:, f, t * P:(t + 1) * P], c.ident[:])
                last.then_inc(toks_done, 1)

            def scores(h, s):
                u = SC + s
                free_tok(h, u)
                for f in range(FH):
                    last = nc.tensor.matmul(tok_ps[:, u % 2, s * P:], kT[:, f, s * P:(s + 1) * P], qT[:, f, s * P:SEQ],
                                            start=(f == 0), stop=(f == FH - 1))
                last.then_inc(toks_done, 1)

            def sample_q(h, b):
                if b == 0:
                    pe.wait_ge(kq_ready, h + 1)
                    need(pe, sn_taken, h)
                for g in range(2):
                    pe.wait_ge(new_ready, PIECES * h + 2 * b + g + 1)
                    for d in range(2):
                        f = 2 * g + d
                        last = nc.tensor.matmul(sn_ps[32 * f:32 * f + 32, :], qm[:, f, 32 * b:32 * b + 32],
                                                state[:, (2 * b + g) % 4, d, :], start=(b == 0), stop=(b == DEC - 1))
                    last.then_inc(sn_used, 1)

            def out_gate(h, t):
                u = OG + t
                if t == 0:
                    pe.wait_ge(og_in, 16 * (h + 1))
                free_tok(h, u)
                p = rows(t)
                for k in range(KT):
                    out, sums = (slice(0, P), 1) if t < NT else (QUADS[k % 4], 4)
                    last = nc.tensor.matmul(tok_ps[out, u % 2, :], c.hT[:, k, t * P:t * P + p], wg[:, k, :],
                                            start=(k < sums), stop=(k >= KT - sums))
                last.then_inc(toks_done, 1)

            def values(h, t):
                u = NUM + t
                free_tok(h, u)
                if t == 0:
                    sem, n = tok_count(h, SC + NT - 1)
                    pe.wait_ge(sem, n)
                    need(pe, n_taken, h)
                    for r in range(NT):
                        for s in range(r + 1):
                            nc.tensor.matmul(q_ps[:, r:r + 1], st[:, s, r * P:(r + 1) * P], one[:], start=(s == 0),
                                             stop=(s == r))
                for s in range(t + 1):
                    last = nc.tensor.matmul(tok_ps[:, u % 2, :], st[:, s, t * P:(t + 1) * P], v[:, s, :],
                                            start=(s == 0), stop=(s == t))
                last.then_inc(toks_done, 1)

            def sample_sum(h):
                free_tok(h, SNUM)
                pe.wait_ge(sn_taken, h + 1)
                nc.tensor.matmul(tok_ps[0:DEC, SNUM % 2, :], sum4[:], sn[:], start=True, stop=True).then_inc(toks_done, 1)

            def prompt_state(h, d):
                u = CP + d
                free_tok(h, u)
                for s in range(NT):
                    last = nc.tensor.matmul(tok_ps[:, u % 2, :], kd[:, s, d * P:(d + 1) * P], v[:, s, :],
                                            start=(s == 0), stop=(s == NT - 1))
                last.then_inc(toks_done, 1)
                if d == 0:
                    sem, n = tok_count(h, NUM + NT - 1)
                    pe.wait_ge(sem, n)
                for s in range(NT):
                    last = nc.tensor.matmul(q_ps[:, FH + d:FH + d + 1], kd[:, s, d * P:(d + 1) * P], one[:],
                                            start=(s == 0), stop=(s == NT - 1))
                if d == FH - 1:
                    last.then_inc(n_done, 1)

            def turned_h(h, t):
                u = HT + t
                p = rows(t)
                free_tok(h, u)
                need_apart(pe, ln_done, TT * h + t + 1, pe_tick)
                for f in range(FH):
                    last = nc.tensor.transpose(tok_ps[:, u % 2, f * P:f * P + p], og[0:p, t, f * P:(f + 1) * P],
                                               c.ident[0:p, 0:p])
                last.then_inc(toks_done, 1)

            def head(h):
                for f in range(FH):
                    z(h, f)
                pe.wait_ge(blk_ready, h + 1)
                pe.wait_ge(xc_in, 16 * (h + 1))
                for n in range(2):
                    for f in range(FH):
                        qk(h, n, f)
                by_token(h, ROWS, 0, NT)
                by_token(h, ROWS + 1, 1, NT)
                pe.wait_ge(xm_in, 16 * (h + 1))
                for t in range(TT):
                    by_token(h, V + t, 2, t)
                for t in range(NT):
                    turned_k(h, t)
                for s in range(NT):
                    scores(h, s)
                for t in range(TT):
                    out_gate(h, t)
                    if t:
                        sample_q(h, t - 1)
                for t in range(NT):
                    values(h, t)
                    if t == 1:
                        sample_q(h, 4)
                sample_q(h, 5)
                for d in range(FH):
                    prompt_state(h, d)
                    if d == 1:
                        sample_q(h, 6)
                sample_q(h, 7)
                sample_sum(h)
                for t in range(TT):
                    turned_h(h, t)

            pe.wait_ge(consts, 9)
            head(0)
            with pe.Fori(1, M_HEADS) as h:
                head(h)


def build_out(nc, c, io):
    with ExitStack() as ctx:
        m = Mem(nc, ctx)
        w = m.sb("w_out_m", [P, 2, MF, 512])
        x = m.sb("x1", [P, TT, D_MODEL])
        ps = m.ps("y_ps", [P, 4, 512])
        w_in = [m.sem(f"w_in{n}_e") for n in range(4)]
        x_in, done, added, stored, summed = (m.sem(n + "_e") for n in ("x_in", "done", "added", "stored", "summed"))
        block = m.block()

        @block.sync
        def _(sp):
            view = io.m_w_out.rearrange("(f p) n -> p f n", p=P)
            for n in range(2):
                for g in range(2):
                    half = slice(g * MF // 2, (g + 1) * MF // 2)
                    sp.dma_start(w[:, n, half, :], view[:, half, n * 512:(n + 1) * 512]).then_inc(w_in[2 * n + g], 16)
            for t in range(TT):
                sp.wait_ge(added, TT + t + 1)
                dst = io.y_prompt[t * P:(t + 1) * P, :] if t < NT else io.y_sample
                sp.dma_start(dst, x[0:rows(t), t, :]).then_inc(stored, 16)
            sp.wait_ge(stored, 16 * TT)

        @block.scalar
        def _(act):
            act.dma_start(x[:, 0:NT, :], io.x1_p.rearrange("(t p) n -> p t n", p=P)).then_inc(x_in, 16)
            act.dma_start(x[0:DEC, NT, :], io.x1_s).then_inc(x_in, 16)

        @block.vector
        def _(dve):
            chain = Chain(dve, summed)
            dve.wait_ge(x_in, 32)
            for g in range(2 * TT):
                n, t = divmod(g, TT)
                p = rows(t)
                dve.wait_ge(done, g + 1)
                cols = x[0:p, t, n * 512:(n + 1) * 512]
                if t == NT:
                    for j in (1, 2, 3):
                        chain(nc.vector.tensor_tensor(cols, cols, ps[QUADS[j], g % 4, :], ALU.add))
                nc.vector.tensor_tensor(cols, cols, ps[0:p, g % 4, :], ALU.add).then_inc(added, 1)

        @block.tensor
        def _(pe):
            for g in range(2 * TT):
                n, t = divmod(g, TT)
                p = rows(t)
                need(pe, added, g - 3)
                for f in range(MF):
                    if t == 0 and f % (MF // 2) == 0:
                        pe.wait_ge(w_in[2 * n + f // (MF // 2)], 16)
                    out, sums = (slice(0, P), 1) if t < NT else (QUADS[f % 4], 4)
                    last = nc.tensor.matmul(ps[out, g % 4, :], c.gated[:, f, t * P:t * P + p], w[:, n, f, :],
                                            start=(f < sums), stop=(f >= MF - sums))
                last.then_inc(done, 1)


class Io:
    pass


class Const:
    pass


def build(nc, io):
    with ExitStack() as ctx:
        ctx.enter_context(nc.allow_non_contiguous_dma(reason="small vectors spread over partitions"))
        m = Mem(nc, ctx)
        c = Const()
        c.ident = m.sb("ident", [P, P])
        c.causal = m.sb("causal", [P, P])
        c.minus_half = m.sb("minus_half", [P, 16])
        build_constants(nc, c)
        c.hT = m.sb("hT", [P, KT, TOK])
        with ExitStack() as layer:
            a = Mem(nc, layer)
            c.smp = a.sb("smp", [DEC, 4, D_MODEL])
            c.oT = a.sb("oT", [P, A_HEADS, TOK])
            build_attention(nc, c, io)
            build_sample_attention_and_out(nc, c, io)
        c.vec = m.sb("vec", [P, 7 * MF])
        c.w_blk = m.sb("w_blk", [P, 3, MF, 4])
        c.in_block = m.sb("in_block", [P, P // 4, 4])
        c.ib_now = m.sb("ib_now", [P, NT])
        build_conv_and_gates(nc, c, io)
        c.gated = m.sb("gated", [P, MF, TOK])
        build_mlstm(nc, c, io)
        build_out(nc, c, io)


_INS = {"x_prompt": (SEQ, D_MODEL), "x_sample": (DEC, D_MODEL), "cache_k": (20, PAGE, D_MODEL),
        "cache_v": (20, PAGE, D_MODEL), "page_table": (1, DEC * NPG), "state_C": (DEC, M_HEADS, M_DIM, M_DIM),
        "state_n": (DEC, M_WIDTH), "state_m": (DEC, M_HEADS), "state_conv": (DEC, CONV - 1, M_WIDTH),
        "a_norm": (D_MODEL,), "a_w_in": (D_MODEL, 4 * D_MODEL), "a_q_norm": (A_DIM,), "a_k_norm": (A_DIM,),
        "a_w_out": (D_MODEL, D_MODEL), "m_norm": (D_MODEL,), "m_w_in": (D_MODEL, 3 * M_WIDTH),
        "m_conv_w": (CONV, M_WIDTH), "m_conv_b": (M_WIDTH,), "m_w_q": (M_WIDTH, 4), "m_w_k": (M_WIDTH, 4),
        "m_w_v": (M_WIDTH, 4), "m_w_if": (3 * M_WIDTH, 2 * M_HEADS), "m_b_if": (2 * M_HEADS,),
        "m_out_norm": (M_WIDTH,), "m_skip": (M_WIDTH,), "m_w_out": (M_WIDTH, D_MODEL)}
_OUTS = {"y_prompt": ((1, SEQ, D_MODEL), (SEQ, D_MODEL)), "y_sample": ((DEC, 1, D_MODEL), (DEC, D_MODEL)),
         "k_prompt": ((1, 1, SEQ, A_HEADS, A_DIM), (SEQ, D_MODEL)),
         "v_prompt": ((1, 1, SEQ, A_HEADS, A_DIM), (SEQ, D_MODEL)),
         "k_sample": ((1, DEC, 1, A_HEADS, A_DIM), (DEC, D_MODEL)),
         "v_sample": ((1, DEC, 1, A_HEADS, A_DIM), (DEC, D_MODEL)),
         "C_prompt": ((1, 1, M_HEADS, M_DIM, M_DIM), (M_HEADS, M_DIM, M_DIM)),
         "n_prompt": ((1, 1, M_HEADS, M_DIM), (M_HEADS, M_DIM)), "m_prompt": ((1, 1, M_HEADS), (M_HEADS, 1)),
         "conv_prompt": ((1, 1, CONV - 1, M_WIDTH), (CONV - 1, M_WIDTH)),
         "C_sample": ((1, DEC, M_HEADS, M_DIM, M_DIM), (DEC, M_HEADS, M_DIM, M_DIM)),
         "n_sample": ((1, DEC, M_HEADS, M_DIM), (DEC, M_WIDTH)), "m_sample": ((1, DEC, M_HEADS), (DEC, M_HEADS)),
         "conv_sample": ((1, DEC, CONV - 1, M_WIDTH), (DEC, CONV - 1, M_WIDTH))}
_SCRATCH = {"own_scores": (DEC, A_HEADS), "own_cells": (DEC * A_HEADS, 1), "q_rows": (DEC, D_MODEL), "x1_p": (SEQ, D_MODEL), "x1_s": (DEC, D_MODEL),
            "xm_keep": (M_HEADS, P, FH, TOK), "xc_keep": (M_HEADS, P, FH, TOK), "v_rows": (M_HEADS, DEC * M_DIM),
            "gate_rows": (3, M_HEADS, SEQ), "step_rows": (3, M_HEADS, DEC)}


def kernel(**inputs):
    import numpy as _np
    import concourse.bacc as _bacc
    from concourse import mybir as _mybir
    from concourse.bass_utils import run_bass_kernel_spmd as _run

    nc = _bacc.Bacc("TRN2", target_bir_lowering=False, num_devices=1)
    arrays, io = {}, Io()
    for name, shape in _INS.items():
        a = _np.ascontiguousarray(inputs[name]).reshape(shape)
        arrays[f"in_{name}"] = a
        io.__dict__[name] = nc.dram_tensor(f"in_{name}", shape, _mybir.dt.from_np(a.dtype), kind="ExternalInput").ap()
    half = A_DIM // 2
    inv = (_np.float32(10000.0) ** (-_np.arange(half, dtype=_np.float32) / _np.float32(half))).astype(_np.float32)
    pos = _np.full(TT * P, PAST, _np.float32)
    pos[:SEQ] = _np.arange(SEQ)
    ang = pos[:, None] * inv[None, :]
    arrays["in_rope"] = _np.stack([_np.concatenate([_np.cos(ang), _np.cos(ang)], 1),
                                   _np.concatenate([-_np.sin(ang), _np.sin(ang)], 1)]).astype(_np.float32)
    io.rope = nc.dram_tensor("in_rope", (2, TT * P, A_DIM), F32, kind="ExternalInput").ap()
    for name, (_, shape) in _OUTS.items():
        io.__dict__[name] = nc.dram_tensor(f"out_{name}", shape, F32, kind="ExternalOutput").ap()
    for name, shape in _SCRATCH.items():
        io.__dict__[name] = nc.dram_tensor(f"keep_{name}", shape, F32, kind="Internal").ap()
    build(nc, io)
    r = _run(nc, [arrays], core_ids=[0])
    return tuple(r.results[0][f"out_{name}"].reshape(shape) for name, (shape, _) in _OUTS.items())
```
